# Optimizing a Trainium2 kernel written in Bass

```python
import jax, jax.numpy as jnp
from jax import lax
import numpy as np

D_MODEL = 1024
BATCH = 1
SEQ = 512
DEPTH = 1
DEC_BATCH = 8
DEC_SEQ = 1
PAST_LEN = 4096
PAGE_SIZE = 128

D_CONV = D_MODEL
CONV_K = 31
GLA_HEADS = 4
GLA_DK = D_MODEL // 2
GLA_DV = D_MODEL
GLA_HK = GLA_DK // GLA_HEADS
GLA_HV = GLA_DV // GLA_HEADS
GLA_RANK = 16
GLA_TAU = 16.0
GLA_CHUNK = 64
D_FF = ((8 * D_MODEL // 3 + 255) // 256) * 256
N_ADA = 9
EPS = 1e-6
IN_SPLITS = (D_CONV, D_CONV, GLA_DK, GLA_DK, GLA_DV, GLA_DV, GLA_RANK, D_MODEL, D_MODEL)
N_IN = sum(IN_SPLITS)

kernel_name = 'hybrid_conformer_gla_decoder_step'

def rms_norm(x, g):
    xf = x.astype(jnp.float32)
    y = xf * lax.rsqrt(jnp.mean(xf * xf, axis=-1, keepdims=True) + EPS)
    return (y * g.astype(jnp.float32)).astype(x.dtype)

def layer_norm(x, g, b):
    xf = x.astype(jnp.float32)
    mu = jnp.mean(xf, axis=-1, keepdims=True)
    var = jnp.mean(jnp.square(xf - mu), axis=-1, keepdims=True)
    y = (xf - mu) * lax.rsqrt(var + EPS) * g.astype(jnp.float32) + b.astype(jnp.float32)
    return y.astype(x.dtype)

def modulate(h, shift, scale):
    return h * (1 + scale[:, None, :]) + shift[:, None, :]

def swiglu(h, w_gate, w_up, w_down):
    return (jax.nn.silu(h @ w_gate) * (h @ w_up)) @ w_down

def causal_depthwise_conv(u, buf, w, b):
    upad = jnp.concatenate([buf.astype(u.dtype), u], axis=1)
    y = lax.conv_general_dilated(upad, w[:, None, :].astype(u.dtype), window_strides=(1,), padding='VALID',
                                 dimension_numbers=('NWC', 'WIO', 'NWC'), feature_group_count=u.shape[-1])
    return y + b, upad[:, -(CONV_K - 1):]

def gla_chunked(q, k, v, log_a, s0):
    bsz, t_len, n_h, _ = q.shape
    blk = min(GLA_CHUNK, t_len)
    n_c = -(-t_len // blk)
    pad = n_c * blk - t_len

    def prep(a):
        a = jnp.pad(a.astype(jnp.float32), ((0, 0), (0, pad), (0, 0), (0, 0)))
        return a.reshape(bsz, n_c, blk, n_h, a.shape[-1]).transpose(1, 0, 3, 2, 4)

    mask = jnp.tril(jnp.ones((blk, blk), dtype=bool))

    def step(s, inp):
        qc, kc, vc, lac = inp
        bc = jnp.cumsum(lac, axis=2)
        o_inter = jnp.einsum('bhtk,bhkv->bhtv', qc * jnp.exp(bc), s)
        diff = bc[:, :, :, None, :] - bc[:, :, None, :, :]
        decay = jnp.exp(jnp.where(mask[:, :, None], diff, -jnp.inf))
        scores = jnp.einsum('bhtk,bhsk,bhtsk->bhts', qc, kc, decay)
        o_intra = jnp.einsum('bhts,bhsv->bhtv', scores, vc)
        b_last = bc[:, :, -1:, :]
        s_new = jnp.exp(b_last[:, :, 0, :, None]) * s + jnp.einsum('bhsk,bhsv->bhkv', kc * jnp.exp(b_last - bc), vc)
        return s_new, o_inter + o_intra

    s_fin, o = lax.scan(step, s0.astype(jnp.float32), (prep(q), prep(k), prep(v), prep(log_a)))
    o = o.transpose(1, 0, 3, 2, 4).reshape(bsz, n_c * blk, n_h, v.shape[-1])[:, :t_len]
    return o, s_fin

def decoder(x, c, conv_state, gla_state, w_ada, b_ada, norm_ffn1, ffn1_gate, ffn1_up, ffn1_down,
            norm_mix, w_in, conv_w, conv_b, conv_ln_g, conv_ln_b, w_conv_out, w_alpha, b_alpha,
            gla_norm, w_gla_out, w_out, norm_ffn2, ffn2_gate, ffn2_up, ffn2_down,
            norm_final, w_ada_final, b_ada_final):
    bsz, t_len, _ = x.shape
    c_act = jax.nn.silu(c)
    split_idx = np.cumsum(IN_SPLITS)[:-1]
    new_conv, new_gla = [], []
    for i in range(DEPTH):
        mod = c_act @ w_ada[i] + b_ada[i]
        sh1, sc1, gt1, sh2, sc2, gt2, sh3, sc3, gt3 = jnp.split(mod, N_ADA, axis=-1)
        h = modulate(rms_norm(x, norm_ffn1[i]), sh1, sc1)
        x = x + 0.5 * gt1[:, None, :] * swiglu(h, ffn1_gate[i], ffn1_up[i], ffn1_down[i])
        h = modulate(rms_norm(x, norm_mix[i]), sh2, sc2)
        z = h @ w_in[i]
        ca, cb, q, k, v, r, a_lr, g_conv, g_gla = jnp.split(z, split_idx, axis=-1)
        u = ca * jax.nn.sigmoid(cb)
        d, conv_new = causal_depthwise_conv(u, conv_state[i], conv_w[i], conv_b[i])
        y_conv = jax.nn.silu(layer_norm(d, conv_ln_g[i], conv_ln_b[i])) @ w_conv_out[i]
        log_a = jax.nn.log_sigmoid((a_lr @ w_alpha[i] + b_alpha[i]).astype(jnp.float32)) / GLA_TAU
        qh = q.reshape(bsz, t_len, GLA_HEADS, GLA_HK) * (GLA_HK ** -0.5)
        kh = k.reshape(bsz, t_len, GLA_HEADS, GLA_HK)
        vh = v.reshape(bsz, t_len, GLA_HEADS, GLA_HV)
        lah = log_a.reshape(bsz, t_len, GLA_HEADS, GLA_HK)
        o, s_new = gla_chunked(qh, kh, vh, lah, gla_state[i])
        o = rms_norm(o, gla_norm[i].reshape(GLA_HEADS, GLA_HV)).reshape(bsz, t_len, GLA_DV).astype(x.dtype)
        y_gla = (o * jax.nn.silu(r)) @ w_gla_out[i]
        merged = jax.nn.sigmoid(g_conv) * y_conv + jax.nn.sigmoid(g_gla) * y_gla
        x = x + gt2[:, None, :] * (merged @ w_out[i])
        h = modulate(rms_norm(x, norm_ffn2[i]), sh3, sc3)
        x = x + 0.5 * gt3[:, None, :] * swiglu(h, ffn2_gate[i], ffn2_up[i], ffn2_down[i])
        new_conv.append(conv_new.astype(conv_state.dtype))
        new_gla.append(s_new.astype(gla_state.dtype))
    shf, scf = jnp.split(c_act @ w_ada_final + b_ada_final, 2, axis=-1)
    y = modulate(rms_norm(x, norm_final), shf, scf)
    return y, jnp.stack(new_conv), jnp.stack(new_gla)

def setup_inputs(seed: int = 0) -> dict:
    key = jax.random.key(seed)
    ks = jax.random.split(key, 40)

    def nrm(k, shape, scale):
        return jax.random.normal(k, shape, dtype=jnp.float32) * scale

    def gain(k, shape):
        return 1.0 + nrm(k, shape, 0.02)

    L = DEPTH
    return {
        'x_prompt': nrm(ks[0], (BATCH, SEQ, D_MODEL), 1.0),
        'x_sample': nrm(ks[1], (DEC_BATCH, DEC_SEQ, D_MODEL), 1.0),
        'c_prompt': nrm(ks[2], (BATCH, D_MODEL), 1.0),
        'c_sample': nrm(ks[3], (DEC_BATCH, D_MODEL), 1.0),
        'state_conv': nrm(ks[4], (L, DEC_BATCH, CONV_K - 1, D_CONV), 0.5),
        'state_gla': nrm(ks[5], (L, DEC_BATCH, GLA_HEADS, GLA_HK, GLA_HV), 0.5),
        'w_ada': nrm(ks[6], (L, D_MODEL, N_ADA * D_MODEL), 0.5 * D_MODEL ** -0.5),
        'b_ada': nrm(ks[7], (L, N_ADA * D_MODEL), 0.01),
        'norm_ffn1': gain(ks[8], (L, D_MODEL)),
        'ffn1_gate': nrm(ks[9], (L, D_MODEL, D_FF), D_MODEL ** -0.5),
        'ffn1_up': nrm(ks[10], (L, D_MODEL, D_FF), D_MODEL ** -0.5),
        'ffn1_down': nrm(ks[11], (L, D_FF, D_MODEL), D_FF ** -0.5),
        'norm_mix': gain(ks[12], (L, D_MODEL)),
        'w_in': nrm(ks[13], (L, D_MODEL, N_IN), D_MODEL ** -0.5),
        'conv_w': nrm(ks[14], (L, CONV_K, D_CONV), CONV_K ** -0.5),
        'conv_b': nrm(ks[15], (L, D_CONV), 0.02),
        'conv_ln_g': gain(ks[16], (L, D_CONV)),
        'conv_ln_b': nrm(ks[17], (L, D_CONV), 0.02),
        'w_conv_out': nrm(ks[18], (L, D_CONV, D_MODEL), D_CONV ** -0.5),
        'w_alpha': nrm(ks[19], (L, GLA_RANK, GLA_DK), GLA_RANK ** -0.5),
        'b_alpha': nrm(ks[20], (L, GLA_DK), 0.1),
        'gla_norm': gain(ks[21], (L, GLA_DV)),
        'w_gla_out': nrm(ks[22], (L, GLA_DV, D_MODEL), GLA_DV ** -0.5),
        'w_out': nrm(ks[23], (L, D_MODEL, D_MODEL), D_MODEL ** -0.5),
        'norm_ffn2': gain(ks[24], (L, D_MODEL)),
        'ffn2_gate': nrm(ks[25], (L, D_MODEL, D_FF), D_MODEL ** -0.5),
        'ffn2_up': nrm(ks[26], (L, D_MODEL, D_FF), D_MODEL ** -0.5),
        'ffn2_down': nrm(ks[27], (L, D_FF, D_MODEL), D_FF ** -0.5),
        'norm_final': gain(ks[28], (D_MODEL,)),
        'w_ada_final': nrm(ks[29], (D_MODEL, 2 * D_MODEL), 0.5 * D_MODEL ** -0.5),
        'b_ada_final': nrm(ks[30], (2 * D_MODEL,), 0.01),
    }

def reference(x_prompt, x_sample, c_prompt, c_sample, state_conv, state_gla,
              w_ada, b_ada, norm_ffn1, ffn1_gate, ffn1_up, ffn1_down,
              norm_mix, w_in, conv_w, conv_b, conv_ln_g, conv_ln_b, w_conv_out, w_alpha, b_alpha,
              gla_norm, w_gla_out, w_out, norm_ffn2, ffn2_gate, ffn2_up, ffn2_down,
              norm_final, w_ada_final, b_ada_final):
    weights = (w_ada, b_ada, norm_ffn1, ffn1_gate, ffn1_up, ffn1_down,
               norm_mix, w_in, conv_w, conv_b, conv_ln_g, conv_ln_b, w_conv_out, w_alpha, b_alpha,
               gla_norm, w_gla_out, w_out, norm_ffn2, ffn2_gate, ffn2_up, ffn2_down,
               norm_final, w_ada_final, b_ada_final)
    bp = x_prompt.shape[0]
    zero_conv = jnp.zeros((DEPTH, bp, CONV_K - 1, D_CONV), dtype=state_conv.dtype)
    zero_gla = jnp.zeros((DEPTH, bp, GLA_HEADS, GLA_HK, GLA_HV), dtype=state_gla.dtype)
    y_prompt, conv_p, gla_p = decoder(x_prompt, c_prompt, zero_conv, zero_gla, *weights)
    y_sample, conv_s, gla_s = decoder(x_sample, c_sample, state_conv, state_gla, *weights)
    return (y_prompt, y_sample, conv_p, gla_p, conv_s, gla_s)


_drawn_inputs = setup_inputs


def setup_inputs(seed=0):
    import zlib

    import numpy as np

    out = dict(_drawn_inputs(seed))
    spreads = {}
    factors = {'norm_ffn1': 8.0,
     'conv_b': 8.0,
     'conv_ln_g': 64.0,
     'conv_ln_b': 64.0,
     'gla_norm': 64.0,
     'norm_ffn2': 22.698,
     'norm_final': 7.582,
     'b_ada_final': 4.214}
    for name, (base, spread) in spreads.items():
        noise = np.random.default_rng([zlib.crc32(name.encode()), seed]).standard_normal(out[name].shape)
        drawn = base * np.exp(spread * noise) if base else spread * noise
        out[name] = __import__('jax').numpy.asarray(drawn.astype(out[name].dtype))
    for name, factor in factors.items():
        out[name] = (out[name] * factor).astype(out[name].dtype)
    return out
```

```python
from contextlib import ExitStack

import numpy as np

import concourse.bass as bass
from concourse import mybir

F32 = mybir.dt.float32
F32R = mybir.dt.float32r
BF16 = mybir.dt.bfloat16
U16 = mybir.dt.uint16
ALU = mybir.AluOpType
ACT = mybir.ActivationFunctionType
AX_X = mybir.AxisListType.X

P = 128
D = 1024
KT = D // P
NP = 512
NS = 8
N = NP + NS
HALF = N // 2
FF = 2816
TAPS = 31
HEADS = 4
DK = 128
DV = 256
RANK = 16
CH = 128
NC = NP // CH
LEVELS = [64, 32, 16, 8, 4, 2, 1]
EPS = 1e-6
UP = TAPS - 1 + N
GROUPS = [8, 8, 6]
W_IN = {"ca": 0, "cb": 1024, "q": 2048, "k": 2560, "v": 3072, "r": 4096, "a": 5120,
        "gc": 5136, "gg": 6160}

VECS = ["norm_ffn1", "norm_mix", "norm_ffn2", "norm_final", "conv_b", "conv_ln_g", "conv_ln_b",
        "gla_norm", "b_alpha"]
VROW = {name: 8 * j for j, name in enumerate(VECS)}
NVEC = 8 * 8 + 4
HIDDEN0 = 2
CONSTS = 32
NADA = 88
(SH1, SC1, GT1, SH2, SC2, GT2, SH3, SC3, GT3, SHF, SCF) = range(11)


class Lin:

    def __init__(self, base, per=0, i=None):
        self.base, self.per, self.i = base, per, i

    def __add__(self, k):
        return Lin(self.base + k, self.per, self.i)

    def half(self):
        return Lin(self.base // 2, self.per // 2, self.i)

    def value(self, mul=1, add=0):
        v = self.base * mul + add
        return v if self.i is None else self.i * (self.per * mul) + v


class Chain:

    def __init__(self, eng, sem):
        self.eng, self.sem, self.n = eng, sem, Lin(0)

    def loop(self, i, per):
        self.n = Lin(self.n.base, per, i)
        self.start = self.n.base

    def end(self, turns):
        assert self.n.base - self.start == self.n.per, (self.n.base - self.start, self.n.per)
        self.n = Lin(self.start + self.n.per * turns)

    def mark(self, ins):
        ins.then_inc(self.sem, 1)
        self.n = self.n + 1

    def wait(self, back=0):
        self.eng.wait_ge(self.sem, self.n.value(add=-back))

    def link(self, ins):
        self.mark(ins)
        self.wait()


def bodies(eng, count, peel):
    if peel:
        yield None, 0
    with eng.Fori(0, count - peel) as i:
        yield i, peel


ADA0 = 10
ADA_SLABS = NADA // 2
ADA_UP = [ADA0, ADA0 + GROUPS[0] + 4, ADA0 + GROUPS[0] + GROUPS[1] + 8]
ADA_DOWN = [ADA_UP[g] + GROUPS[g] for g in range(3)]


def plan():
    at, n = {}, 0
    for name, units in ([(f"{w}1_{g}", u) for g in range(3) for w, u in (("up", GROUPS[g] * 2), ("down", 8))]
                        + [("conv", 16), ("alr", 4), ("qk", 8), ("v", 8), ("gates", 24),
                           ("yconv", 8), ("ygla", 8), ("out", 8)]
                        + [(f"{w}2_{g}", u) for g in range(3) for w, u in (("up", GROUPS[g] * 2), ("down", 8))]):
        at[name] = n
        n += units
    return at, n


def decoder_step(nc, a, o):
    at, UNITS = plan()
    A = {k: v for k, v in a.items()}

    with ExitStack() as ctx:
        def sb(name, shape, dt=F32):
            return ctx.enter_context(nc.sbuf_tensor(name, shape, dt))

        def overlay(*views):
            out = []
            for name, shape, dt in views[:-1]:
                with nc.sbuf_tensor(name, shape, dt) as t:
                    out.append(t)
            name, shape, dt = views[-1]
            out.append(sb(name, shape, dt))
            return out

        def sem(name):
            return ctx.enter_context(nc.semaphore(name))

        raw = sb("raw", [P, 2, KT, 256])
        w_hi = [sb(f"w_hi{p}", [P, KT, P], F32R) for p in range(2)]
        w_lo = [sb(f"w_lo{p}", [P, KT, P], F32R) for p in range(2)]
        h_hi = sb("h_hi", [P, KT, N], F32R)
        h_lo = sb("h_lo", [P, KT, N], F32R)
        x = sb("x", [P, KT, N])
        BF = 2 * KT * N
        lay = {}
        off = 0
        for name, cols in (("E", 2 * NP), ("M", 2 * N), ("EB", N), ("QS", NP), ("SC", NP), ("KTK", NP),
                           ("VH", NC * DV), ("SB", NC * DV), ("ST", NS * DV)):
            lay[name] = (off, off + cols)
            off += cols
        assert off <= BF
        f_hl = []
        with ExitStack() as c2:
            for nm in ("f_hi", "f_lo"):
                f_hl.append(c2.enter_context(nc.sbuf_tensor(nm, [P, KT, N], F32R)))
        f_hi, f_lo = f_hl
        work = sb("work", [P, BF])

        def wk(name):
            return work[:, lay[name][0]:lay[name][1]]

        E_ = wk("E").rearrange("p (b n) -> p b n", b=2)
        M_ = wk("M").rearrange("p (b n) -> p b n", b=2)
        EB = wk("EB")
        QS = wk("QS")
        SC = wk("SC")
        KTK = wk("KTK").rearrange("p (c n) -> p c n", c=NC)
        VH = wk("VH").rearrange("p (c n) -> p c n", c=NC)
        SB = wk("SB").rearrange("p (c n) -> p c n", c=NC)
        ST = wk("ST").rearrange("p (b n) -> p b n", b=NS)
        work_t = work[:].rearrange("p (t n) -> p t n", t=2 * KT)
        t_gg, t_gc = work_t[:, 0:KT, :], work_t[:, KT:, :]

        wa0, qk = overlay(("wa0", [P, 2, KT, 256], F32R), ("qk", [P, KT, N], F32))
        xtok, raw_a2, convs, vtok, ytok, o_lo = overlay(
            ("xtok", [P, 4, D], F32), ("raw_a2", [P, 2, KT, 256], F32), ("convs", [P, 2 * D + KT * NS * TAPS], F32),
            ("vtok", [P, NC, D], F32), ("ytok", [P, 4, D], F32), ("o_lo", [P, KT, N], F32R))
        rows, wa1, o_hi, u = overlay(("rows", [P, 2 * D + 4 * P], F32), ("wa1", [P, 2, KT, 256], F32R),
                                ("o_hi", [P, KT, N], F32R),
                                ("u", [P, KT, UP], F32))
        raw_a, d = overlay(("raw_a", [P, 2, KT, 256], F32), ("d", [P, KT, N], F32))
        lb = sb("lb", [P, HEADS, N])
        wa = [wa0, wa1]
        rows_a = lb[0:20, 0:2, 0:256]
        sg = sb("sg", [P, 4, N])
        mod = sb("mod", [P, NADA, 10])
        vt = sb("vt", [P, NVEC + NADA])
        cw = sb("cw", [P, TAPS * KT])
        qk_scale = sb("qk_scale", [P, 2])
        masks = sb("masks", [P, len(LEVELS) + 1, P], BF16)
        ident = sb("ident", [P, P])
        ones = sb("ones", [P, P])
        sel = sb("sel", [20, 10])
        eps = sb("eps", [P, 1])
        c_f = sb("c_f", [P, KT, 10])
        c_hl = sb("c_hl", [P, KT, 20], F32R)
        t8 = sb("t8", [P, 2, NS])
        hs = sb("hs", [P, KT, NS])
        ks8 = sb("ks8", [NS, DK])
        walpha, alr = work[0:RANK, 0:HEADS * DK], work[0:RANK, HEADS * DK:HEADS * DK + N]
        x_rows = x[0:NS, 0:4, :].rearrange("p a n -> p (a n)")
        vs, km = x_rows[:, 0:D], x_rows[:, D:2 * D].rearrange("p (b n) -> p b n", b=NS)
        x_rows_d = nc.dram_tensor("x_rows_d", [NS, 4 * N], F32, kind="Internal").ap()
        ysrow = d[0:NS, 0:2, :].rearrange("p a n -> p (a n)")[:, 0:D]
        crow = rows[0:9, 0:D]
        xsrow = rows[0:NS, D:2 * D]
        vrow = rows[0:NVEC, 2 * D:2 * D + P]
        brow = rows[0:NADA, 2 * D + P:2 * D + 2 * P]
        cwrow = rows[0:TAPS * 4, 2 * D + 2 * P:2 * D + 4 * P].rearrange("p (g n) -> p g n", g=2)
        srow = convs[0:120, 0:2 * D].rearrange("p (g n) -> p g n", g=2)
        sT = convs[:, 2 * D:].rearrange("p (t b j) -> p t b j", t=KT, b=NS)

        def ada_slot(m):
            if m.i is None and m.base < ADA0:
                slot, loads = m.base % 4, Lin(m.base // 4 + 1)
            else:
                slot = m.base % 2
                loads = (m + (-ADA0 - slot)).half() + (ADA0 + 3) // 4 + 1
            return raw_a[:, slot] if slot < 2 else raw_a2[:, slot - 2], s_araw[slot], loads.value(16)

        pu = [ctx.enter_context(nc.psum_tensor(f"pu{p}", [P, 2, 512], F32)) for p in range(2)]
        pg = ctx.enter_context(nc.psum_tensor("pg", [P, 4, 512], F32))

        gates_d = nc.dram_tensor("gates_d", [3, KT, P, N], F32, kind="Internal").ap()

        def sems(**names):
            return {k: sem(v) for k, v in names.items()}

        s_raw = [sem("raw0_loaded"), sem("raw1_loaded")]
        s_free = sem("raw_slabs_found_free")
        s_hi, s_lo, s_done = sem("w_hi_ready"), sem("w_lo_ready"), sem("unit_done")
        s_evac = [sem("even_unit_out_of_psum"), sem("odd_unit_out_of_psum")]
        s_const = sem("consts_ready")
        s_ld = {k: sem("loaded_" + k) for k in ("x", "c", "xs", "vec", "b", "cw", "st", "wa")}
        s_tp, s_te, s_td = sem("start_transposed"), sem("start_read_by_act"), sem("start_read_by_dve")
        s_cf, s_c = sem("c_ready"), sem("c_split")
        s_araw = [sem(f"ada_raw{j}_loaded") for j in range(4)]
        s_afree = sem("ada_slabs_found_free")
        s_wah, s_wal, s_ad = sem("ada_hi_ready"), sem("ada_lo_ready"), sem("ada_rows_in_psum")
        s_ar, s_at, s_mod = sem("ada_rows_ready"), sem("ada_rows_transposed"), sem("modulation_ready")
        s_sq, s_sqf, s_ss = sem("square_ready"), sem("square_added"), sem("sums_in_psum")
        s_root, s_rstd, s_xn = sem("root_ready"), sem("rstd_ready"), sem("x_times_rstd")
        s_hf, s_hh, s_h = sem("h_full"), sem("h_hi_ready"), sem("h_split")
        s_ln = sem("conv_tile_sums")
        s_cen = sem("conv_tile_centered")
        s_ahi, s_a, s_x = sem("hidden_hi_ready"), sem("hidden_split"), sem("x_updated")
        s_ct, s_cts, s_cst = sem("u_tails_transposed"), sem("u_tails_staged"), sem("u_tails_stored")
        s_cvt, s_cve, s_cvs = sem("state_conv_transposed"), sem("state_conv_read"), sem("sample_conv_done")
        s_cv = sem("conv_step")
        s_cpy = sem("state_conv_copied")
        s_xsp, s_xr = sem("x_rows_spilled"), sem("x_rows_restored")
        s_lg, s_z, s_az = sem("logits_ready"), sem("z_ready"), sem("abs_z_ready")
        s_l, s_b = sem("log1p_ready"), sem("b_ready")
        s_vt, s_v = sem("v_transposed"), sem("vtok_ready")
        s_gt = sem("r_tanh_ready")
        s_gsp = [sem(f"gate_spilled{j}") for j in range(4)]
        s_gr = {k: sem("gate_reloaded_" + k) for k in ("r", "gc", "gg")}
        s_gd, s_ge, s_gk = sem("gla_diff_ready"), sem("gla_exp_ready"), sem("gla_v_head_ready")
        s_gm, s_gg, s_gp = sem("gla_mix_ready"), sem("gla_gram_ready"), sem("gla_scores_merged")
        s_merge = sem("gla_scores_free_to_merge")
        s_kt, s_kr, s_km = sem("gla_k_transposed"), sem("gla_k_read"), sem("sample_k_masked")
        s_ds, s_S = sem("gla_ds_ready"), sem("gla_state_ready")
        s_ko, s_sn = sem("sample_outer_ready"), sem("sample_state_ready")
        s_o, s_oe = sem("gla_o_ready"), sem("gla_o_read")
        s_st, s_sto, s_So = sem("state_loaded"), sem("sample_state_stored"), sem("prompt_state_stored")
        s_osq, s_osum, s_os = sem("o_squares_ready"), sem("o_squares_added"), sem("o_sums_in_psum")
        s_om, s_or = sem("o_root_ready"), sem("o_rstd_ready")
        s_ox, s_of, s_oh, s_osp = sem("o_normed"), sem("o_gated"), sem("o_hi_ready"), sem("o_split")
        s_mf, s_mh, s_mp = sem("merged_ready"), sem("merged_hi_ready"), sem("merged_split")
        s_yn, s_yt, s_ye, s_fin = sem("y_ready"), sem("y_transposed"), sem("y_staged"), sem("y_stored")
        s_ys, s_yse = sem("sample_y_ready"), sem("sample_y_staged")
        s_dv, s_ac = sem("dve_step"), sem("act_step")

        block = ctx.enter_context(nc.Block())
        w_ada, w_in = A["w_ada"][0], A["w_in"][0]
        MIX = {"k": 1, "qs": 2, 7: 10} | {l: l + 3 for l in range(7)}

        def flat(v):
            return v.rearrange("p o n -> p (o n)")

        def tile(t, n, a=0, b=N):
            return flat(t[:, bass.ds(n, 1), a:b])

        def halves(v):
            return v.rearrange("p (e n) -> p e n", e=2)

        @block.sync
        def _(sp):
            def cols(w, c, k=KT, r0=0):
                v = w[r0:r0 + k * P, :].rearrange("(k p) n -> p k n", p=P)
                return v[:, :, bass.ds(c if isinstance(c, int) else sp.snap(c), 256)]

            def load(n, slot, src, k=KT):
                if n.i is not None or n.base >= 4:
                    sp.wait_ge(s_lo, n.value(add=-2))
                    sp.sem_inc(s_free, 1)
                sp.dma_start(raw[:, slot, 0:k, :], src).then_inc(s_raw[slot], 16)

            def pair(n, w, c, c2=None, k=KT, r0=0):
                load(n, 0, cols(w, c, k, r0), k)
                w2, c2 = c2 if c2 is not None else (w, c + 256)
                load(n + 2, 1, cols(w2, c2, k, r0), k)

            def ffn(which):
                wg, wu, wd = (A[f"ffn{which}_{w}"][0] for w in ("gate", "up", "down"))
                for g in range(3):
                    r0 = sum(GROUPS[:g]) * P
                    n0 = at[f"up{which}_{g}"]
                    for i, k in bodies(sp, GROUPS[g] // 2, n0 == 0):
                        c = r0 if i is None else i * 256 + (r0 + 256 * k)
                        pair(Lin(n0 + 4 * k, 4, i), wg, c, (wu, c))
                    with sp.Fori(0, 2) as i:
                        pair(Lin(at[f"down{which}_{g}"], 4, i), wd, i * 512, k=GROUPS[g], r0=r0)

            sp.wait_ge(s_ld["x"], 64)
            ffn(1)
            with sp.Fori(0, 4) as i:
                pair(Lin(at["conv"], 4, i), w_in, i * 256 + W_IN["cb"], (w_in, i * 256 + W_IN["ca"]))
            pair(Lin(at["alr"]), w_in, W_IN["a"], (w_in, W_IN["a"]))
            for name, w, c in (("qk", w_in, W_IN["q"]), ("v", w_in, W_IN["v"])):
                with sp.Fori(0, 2) as i:
                    pair(Lin(at[name], 4, i), w, i * 512 + c)
            with sp.Fori(0, 2) as i:
                for j, g in enumerate(("r", "gc", "gg")):
                    pair(Lin(at["gates"] + 4 * j, 12, i), w_in, i * 512 + W_IN[g])
            for name, w in (("yconv", "w_conv_out"), ("ygla", "w_gla_out"), ("out", "w_out")):
                with sp.Fori(0, 2) as i:
                    pair(Lin(at[name], 4, i), A[w][0], i * 512)
            ffn(2)

            yp = o["y_prompt"][0].rearrange("(c p) d -> p c d", p=P)
            for a, b in ((0, 4), (4, 6), (6, 8)):
                sp.wait_ge(s_ye, b)
                sp.dma_start(yp[:, :, a * P:b * P], ytok[:, :, a * P:b * P]).then_inc(s_fin, 16)
            sp.wait_ge(s_yse, 1)
            sp.dma_start(o["y_sample"].rearrange("b t d -> (b t) d"), ysrow).then_inc(s_fin, 16)
            sp.wait_ge(s_fin, 64)

        @block.gpsimd
        def _(pool):
            def ada_load(m, w, c):
                if m.i is not None or m.base >= ADA0:
                    pool.wait_ge(s_wal, m.value(add=-1))
                    pool.sem_inc(s_afree, 1)
                elif m.base >= 4:
                    pool.wait_ge(s_wal, m.base - 3)
                elif m.base >= 2:
                    pool.wait_ge(s_te, 1 + KT)
                dst, s_loaded, _ = ada_slot(m)
                v = w.rearrange("(k p) n -> p k n", p=P)
                pool.dma_start(dst, v[:, :, bass.ds(c, 256)]).then_inc(s_loaded, 16)

            for m in range(2):
                ada_load(Lin(m), w_ada, m * 256)
            nc.gpsimd.memset(ident[:], 0.0).then_inc(s_const, 1)
            nc.gpsimd.memset(ones[:], 1.0).then_inc(s_const, 1)
            nc.gpsimd.memset(masks[:], 0.0).then_inc(s_const, 1)
            nc.gpsimd.memset(eps[:], EPS).then_inc(s_const, 1)
            nc.gpsimd.memset(qk_scale[:, 0:1], DK ** -0.5).then_inc(s_const, 1)
            nc.gpsimd.memset(qk_scale[:, 1:2], 1.0).then_inc(s_const, 1)
            pool.wait_ge(s_const, 6)
            nc.gpsimd.affine_select(out=ident[:], in_=ident[:], compare_op=ALU.not_equal, fill=1.0,
                                    base=0, pattern=[[-1, P]], channel_multiplier=1).then_inc(s_const, 1)
            n = 7
            for l, h in enumerate(LEVELS):
                v = masks[:, l, :].rearrange("p (b e t) -> p b e t", e=2, t=h)
                nc.gpsimd.memset(v[:, :, 1, :], 1.0).then_inc(s_const, 1)
                n += 1
                for base, step in ((0, 1), (h - 1, -1)):
                    pool.wait_ge(s_const, n)
                    nc.gpsimd.affine_select(out=v, in_=v, compare_op=ALU.is_ge, fill=0.0, base=base,
                                            pattern=[[-step * 2 * h, P // (2 * h)], [0, 2], [0, h]],
                                            channel_multiplier=step).then_inc(s_const, 1)
                    n += 1
            nc.gpsimd.affine_select(out=masks[:, 7, :], in_=masks[:, 7, :], compare_op=ALU.not_equal,
                                    fill=1.0, base=0, pattern=[[-1, P]], channel_multiplier=1
                                    ).then_inc(s_const, 1)
            nc.gpsimd.memset(sel[:], 0.0).then_inc(s_const, 1)
            for j in range(2):
                pool.wait_ge(s_const, CONSTS - 2 + j)
                nc.gpsimd.affine_select(out=sel[:], in_=sel[:], compare_op=ALU.not_equal, fill=1.0,
                                        base=-10 * j, pattern=[[-1, 10]], channel_multiplier=1).then_inc(s_const, 1)
            assert n + 4 == CONSTS
            for m in range(2, ADA0):
                ada_load(Lin(m), w_ada, m * 256)
            with pool.Fori(0, (36 - ADA0) // 2) as i:
                for j in range(2):
                    ada_load(Lin(ADA0 + j, 2, i), w_ada, i * 512 + 256 * (ADA0 + j))
            with pool.Fori(0, 4) as i:
                for j in range(2):
                    ada_load(Lin(36 + j, 2, i), A["w_ada_final"], i * 512 + 256 * j)

            pool.dma_start(o["conv_s"][0, :, 0:TAPS - 2, :], A["state_conv"][0, :, 1:TAPS - 1, :]
                           ).then_inc(s_cpy, 16)
            rows_st = A["state_conv"][0].rearrange("(g b) j f -> g (b j) f", g=2)
            for g in range(2):
                pool.dma_start(convs[0:120, g * D:(g + 1) * D], rows_st[g]).then_inc(s_ld["st"], 16)
            st_in = A["state_gla"][0].rearrange("b h k v -> h k b v")
            st_out = o["gla_s"][0].rearrange("b h k v -> h k b v")
            pool.wait_ge(s_done, at["conv"])
            pool.dma_start(walpha, A["w_alpha"][0]).then_inc(s_ld["wa"], 16)
            pool.dma_start(ST, st_in[0]).then_inc(s_st, 16)
            pool.wait_ge(s_x, 3 * KT)
            pool.dma_start(x_rows_d, x_rows).then_inc(s_xsp, 16)
            pool.wait_ge(s_cts, 1)
            pool.dma_start(o["conv_p"][0, 0], flat(sg[:])[0:TAPS - 1, 0:D]).then_inc(s_cst, 16)
            pool.dma_start(o["conv_s"][0, :, TAPS - 2, :], flat(sg[:])[TAPS - 1:TAPS - 1 + NS, 0:D]
                           ).then_inc(s_cst, 16)
            for h in range(HEADS):
                pool.wait_ge(s_S, 4 * h + 4)
                pool.dma_start(o["gla_p"][0, 0, h], SB[:, 3, :]).then_inc(s_So, 16)
                pool.wait_ge(s_oe, 2 * h + 1)
                pool.dma_start(st_out[h], ST).then_inc(s_sto, 16)
                pool.wait_ge(s_So, 16 * (h + 1))
                pool.wait_ge(s_sto, 16 * (h + 1))
                if h + 1 < HEADS:
                    pool.dma_start(ST, st_in[h + 1]).then_inc(s_st, 16)
            pool.wait_ge(s_oe, 2 * HEADS)
            pool.wait_ge(s_xsp, 16)
            pool.dma_start(x_rows, x_rows_d).then_inc(s_xr, 16)
            for j in range(4):
                pool.wait_ge(s_gsp[j], 6 * 16)
            back = [gates_d[j].rearrange("t p n -> p t n") for j in range(3)]
            pool.dma_start(t_gc, back[1]).then_inc(s_gr["gc"], 16)
            pool.wait_ge(s_h, 3 * KT)
            pool.dma_start(d[:], back[0]).then_inc(s_gr["r"], 16)
            pool.dma_start(t_gg, back[2]).then_inc(s_gr["gg"], 16)
            pool.wait_ge(s_cst, 32)
            pool.wait_ge(s_cpy, 16)

        @block.tensor
        def _(pe):
            mm = nc.tensor.matmul

            def weights_and_psum(n, p):
                pe.wait_ge(s_lo, n.value(add=1))
                if n.i is not None or n.base >= 2:
                    pe.wait_ge(s_evac[p], n.half().value())

            def unit(n, p, hi, lo, k_tiles=KT, ready=None, done=1):
                weights_and_psum(n, p)
                for k in range(k_tiles):
                    if ready is not None:
                        s, v, first = ready
                        if k == 0 and first > 1:
                            pe.wait_ge(s, v + first)
                        elif k >= first or k == 0:
                            pe.wait_ge(s, v + k + 1)
                    for j, (w, m) in enumerate(((w_hi, hi), (w_hi, lo), (w_lo, hi))):
                        for e in range(2):
                            last = mm(pu[p][:, e, 0:HALF], w[p][:, k, :], m[:, k, e * HALF:(e + 1) * HALF],
                                      start=(k == 0 and j == 0), stop=(k == k_tiles - 1 and j == 2))
                last.then_inc(s_done, done)

            def ada(m):
                slot = m.base % 2
                if m.i is not None or m.base >= 2:
                    pe.wait_ge(s_ar, m.value(add=-1))
                pe.wait_ge(s_wal, m.value(1, 1))
                for k in range(KT):
                    for j in range(2):
                        last = mm(pg[0:20, 2 + slot, 0:256], c_hl[:, k, :], wa[slot][:, j, k, :],
                                  start=(k == 0 and j == 0), stop=(k == KT - 1 and j == 1))
                last.then_inc(s_ad, 1)

            def ada_transpose(m):
                slot = m.base % 2
                if m.i is not None or m.base >= 2:
                    pe.wait_ge(s_mod, m.value(add=-1))
                pe.wait_ge(s_ar, m.value(1, 1))
                for e in range(2):
                    last = mm(pg[:, slot, 10 * e:10 * e + 10], rows_a[:, slot, e * P:(e + 1) * P], sel[:],
                              start=True, stop=True)
                last.then_inc(s_at, 1)

            def sums(src, b=0):
                for e in range(2):
                    last = mm(pg[:, b + e, 0:HALF], ones[:], src[:, e * HALF:(e + 1) * HALF],
                              start=True, stop=True)
                return last

            def norm_sums(q):
                pe.wait_ge(s_sqf, KT * (q + 1))
                sums(sg[:, 2, :]).then_inc(s_ss, 1)

            pe.wait_ge(s_const, CONSTS)
            pe.wait_ge(s_ld["c"], 32)
            for t in range(KT):
                last = nc.tensor.transpose(pg[:, 0, 10 * t:10 * t + 9], crow[:, t * P:(t + 1) * P], ident[0:9, 0:9])
            last.then_inc(s_tp, 1)
            pe.wait_ge(s_ld["vec"], 16 * len(VECS))
            pe.wait_ge(s_ld["b"], 32)
            pe.wait_ge(s_ld["cw"], 32)
            nc.tensor.transpose(pg[:, 1, 0:NVEC], vrow, ident[0:NVEC, 0:NVEC])
            nc.tensor.transpose(pg[:, 1, NVEC:NVEC + NADA], brow, ident[0:NADA, 0:NADA])
            for g in range(2):
                last = nc.tensor.transpose(pg[:, 1, 160 + g * 124:160 + g * 124 + 124], cwrow[:, g, :],
                                           ident[0:124, 0:124])
            last.then_inc(s_tp, 1)
            pe.wait_ge(s_ld["x"], 64)
            pe.wait_ge(s_ld["xs"], 16)
            for t in range(KT):
                b = t % 2
                if t >= 2:
                    pe.wait_ge(s_te, t)
                    pe.wait_ge(s_td, t)
                for c in range(4):
                    nc.tensor.transpose(pg[:, 2 + b, c * P:(c + 1) * P], xtok[:, c, t * P:(t + 1) * P], ident[:])
                if t == 0:
                    pe.wait_ge(s_te, 1)
                if t == 1:
                    pe.wait_ge(s_td, 1)
                nc.tensor.transpose(pg[:, b, 0:NS], xsrow[:, t * P:(t + 1) * P], ident[0:NS, 0:NS]
                                    ).then_inc(s_tp, 1)
            pe.wait_ge(s_c, 2)
            pe.wait_ge(s_te, 1 + KT)
            pe.wait_ge(s_td, 1 + KT)
            norm_sums(0)
            for m in range(ADA0):
                ada(Lin(m))
                if m == 0:
                    pe.wait_ge(s_rstd, 1)
                ada_transpose(Lin(m))

            def ffn(which):
                def ada_part(c, m, i):
                    if which == 1:
                        (ada_transpose if c % 2 else ada)(Lin(m + c // 2, 2, i))

                for g in range(3):
                    n0 = at[f"up{which}_{g}"]
                    for i, k in bodies(pe, GROUPS[g] // 2, n0 == 0):
                        for c in range(4):
                            unit(Lin(n0 + 4 * k + c, 4, i), c % 2, h_hi, h_lo,
                                 ready=(s_h, (which - 1) * 3 * KT, 1) if c == 0 else None)
                            ada_part(c, ADA_UP[g] + 2 * k, i)
                    a0 = HIDDEN0 + (which - 1) * (FF // P) + sum(GROUPS[:g])
                    with pe.Fori(0, 2) as i:
                        for c in range(4):
                            unit(Lin(at[f"down{which}_{g}"] + c, 4, i), c % 2, f_hi, f_lo, GROUPS[g],
                                 ready=(s_a, a0, GROUPS[g] - 1) if c == 0 else None)
                            ada_part(c, ADA_DOWN[g], i)

            ffn(1)
            pe.wait_ge(s_mod, ADA_SLABS)
            norm_sums(1)

            pe.wait_ge(s_ld["st"], 32)
            pe.wait_ge(s_rstd, 2)
            for t in range(KT):
                if t >= 4:
                    pe.wait_ge(s_cve, t - 3)
                for g in range(2):
                    last = nc.tensor.transpose(pg[:, t % 4, g * 120:(g + 1) * 120],
                                               convs[0:120, g * D + t * P:g * D + (t + 1) * P], ident[0:120, 0:120])
                last.then_inc(s_cvt, 1)
            with pe.Fori(0, 4) as i:
                for c in range(4):
                    unit(Lin(at["conv"] + c, 4, i), c % 2, h_hi, h_lo,
                         ready=(s_h, KT, 1) if c == 0 else None)
            n = at["alr"]
            pe.wait_ge(s_evac[1], n // 2)
            unit(Lin(n), 0, h_hi, h_lo, done=4)
            pe.wait_ge(s_cve, KT)
            pe.wait_ge(s_evac[1], n // 2)
            for t in range(KT):
                last = nc.tensor.transpose(pg[0:TAPS - 1 + NS, t // 4, (t % 4) * P:(t % 4 + 1) * P],
                                           u[:, t, NP:UP], ident[:])
            last.then_inc(s_ct, 1)
            pe.wait_ge(s_evac[0], n // 2 + 2)
            pe.wait_ge(s_ld["wa"], 16)
            for h in range(HEADS):
                b = 2 * (h % 2)
                if h == 0:
                    pe.wait_ge(s_cts, 1)
                elif h >= 2:
                    pe.wait_ge(s_z, h - 1)
                for e in range(2):
                    last = mm(pg[:, b + e, 0:HALF], walpha[:, h * DK:(h + 1) * DK],
                              alr[:, e * HALF:(e + 1) * HALF], start=True, stop=True)
                last.then_inc(s_lg, 1)
            with pe.Fori(0, 2) as i:
                for c in range(4):
                    unit(Lin(at["qk"] + c, 4, i), c % 2, h_hi, h_lo)
            pe.wait_ge(s_z, HEADS)
            with pe.Fori(0, 2) as i:
                for c in range(4):
                    unit(Lin(at["v"] + c, 4, i), c % 2, h_hi, h_lo)
                for e in range(2):
                    nn = Lin(at["v"] + 2 + e, 4, i)
                    pe.wait_ge(s_evac[e], nn.half().value(add=1))
                for e in range(2):
                    if e:
                        pe.wait_ge(s_v, i * 2 + 1)
                    for t in range(2):
                        for c in range(NC):
                            q = c * DV + t * P
                            nc.tensor.transpose(pg[:, q // 512, q % 512:q % 512 + P],
                                                sg[:, 2 * e + t, c * CH:(c + 1) * CH], ident[:])
                        last = nc.tensor.transpose(pg[0:NS, 2, t * P:(t + 1) * P], sg[:, 2 * e + t, NP:N], ident[:])
                    last.then_inc(s_vt, 1)
                pe.wait_ge(s_v, i * 2 + 2)

            def gram(h, l, rhs=None):
                pe.wait_ge(s_gm, h.value(10, MIX[l]))
                if l >= 2:
                    pe.wait_ge(s_gp, h.value(8, l - 1))
                for c in range(NC):
                    m = M_[:, l % 2, c * CH:(c + 1) * CH]
                    last = mm(pg[:, l % 2, c * CH:(c + 1) * CH], m,
                              m if rhs is None else rhs[:, c * CH:(c + 1) * CH], start=True, stop=True)
                last.then_inc(s_gg, 1)

            def k_transposes(h):
                pe.wait_ge(s_gm, h.value(10, MIX["k"]))
                for c in range(NC):
                    nc.tensor.transpose(pg[:, 2, c * CH:(c + 1) * CH], M_[:, 0, c * CH:(c + 1) * CH], ident[:])
                nc.tensor.transpose(pg[0:NS, 3, 0:DK], M_[:, 0, NP:N], ident[:]).then_inc(s_kt, 1)

            def chunk_states(h):
                pe.wait_ge(s_kr, h.value(2, 2))
                pe.wait_ge(s_gk, h.value(1, 1))
                for c in range(NC):
                    last = mm(pg[:, 2 + c // 2, (c % 2) * DV:(c % 2 + 1) * DV], KTK[:, c, :], VH[:, c, :],
                              start=True, stop=True)
                last.then_inc(s_ds, 1)

            def outer_ready(h, r):
                pe.wait_ge(s_km, h.value(1, 1))
                if r == 0:
                    pe.wait_ge(s_S, h.value(4, 4))
                else:
                    pe.wait_ge(s_sn, h.value(8, 4))

            def sample_outer(h, r):
                for b in range(4):
                    last = mm(pg[:, 2 + b // 2, (b % 2) * DV:(b % 2 + 1) * DV], km[:, 4 * r + b, :],
                              vs[:, bass.ds(h.value(DV), DV)], start=True, stop=True)
                last.then_inc(s_ko, 1)

            def sample_o(h):
                pe.wait_ge(s_sn, h.value(8, 8))
                q = tile(qk, h.value(2))
                for t in range(2):
                    for b in range(NS):
                        last = mm(pg[:, 2, t * NS + b:t * NS + b + 1], ST[:, b, t * P:(t + 1) * P],
                                  q[:, NP + b:NP + b + 1], start=True, stop=True)
                last.then_inc(s_o, 1)

            def prompt_o(h):
                pe.wait_ge(s_gp, h.value(8, 8))
                pe.wait_ge(s_oe, h.value(2, 1))
                for t in range(2):
                    for c in range(NC):
                        cs, ts = slice(c * CH, (c + 1) * CH), slice(t * P, (t + 1) * P)
                        last = mm(pg[:, 2 + t, cs], VH[:, c, ts], SC[:, cs], start=True, stop=(c == 0))
                        if c:
                            last = mm(pg[:, 2 + t, cs], SB[:, c - 1, ts], QS[:, cs], start=False, stop=True)
                last.then_inc(s_o, 1)

            with pe.Fori(0, 2) as i:
                for hh in range(2):
                    h = Lin(hh, 2, i)
                    for s in range(6):
                        unit(Lin(at["gates"] + 6 * hh + s, 12, i), s % 2, h_hi, h_lo)
                        if s == 1:
                            k_transposes(h)
                        if s == 2:
                            chunk_states(h)
                            gram(h, 0)
                            gram(h, 1)
                        if s == 3:
                            outer_ready(h, 0)
                            gram(h, 2)
                            sample_outer(h, 0)
                            gram(h, 3)
                        if s == 4:
                            outer_ready(h, 1)
                            gram(h, 4)
                            sample_outer(h, 1)
                            gram(h, 5)
                        if s == 5:
                            sample_o(h)
                            gram(h, 6)
                            gram(h, 7, tile(qk, h.value(2)))
                            prompt_o(h)

            pe.wait_ge(s_ln, KT)
            pe.wait_ge(s_oe, 2 * HEADS)
            sums(sg[:, 2, :]).then_inc(s_ss, 1)
            norm_sums(2)
            for h in range(HEADS):
                pe.wait_ge(s_osum, h + 1)
                if h == 0:
                    pe.wait_ge(s_rstd, 3)
                if h >= 2:
                    pe.wait_ge(s_or, h - 1)
                sums(lb[:, h, :], 2 * (h % 2)).then_inc(s_os, 1)
            for name, hi, lo, s, v in (("yconv", h_hi, h_lo, s_h, 2 * KT), ("ygla", o_hi, o_lo, s_osp, 0),
                                       ("out", h_hi, h_lo, s_mp, 0)):
                with pe.Fori(0, 2) as i:
                    for c in range(4):
                        unit(Lin(at[name] + c, 4, i), c % 2, hi, lo, ready=(s, v, 1) if c == 0 else None)
            norm_sums(3)
            ffn(2)
            norm_sums(4)
            pe.wait_ge(s_ys, 1)
            for t in range(KT):
                last = nc.tensor.transpose(pu[0][0:NS, t // 4, (t % 4) * P:(t % 4 + 1) * P], x[:, t, NP:N], ident[:])
            last.then_inc(s_yt, 1)
            for t in range(KT):
                pe.wait_ge(s_yn, t + 1)
                if t >= 4:
                    pe.wait_ge(s_ye, t - 3)
                for c in range(4):
                    last = nc.tensor.transpose(pg[:, t % 4, c * P:(c + 1) * P], x[:, t, c * P:(c + 1) * P], ident[:])
                last.then_inc(s_yt, 1)

        @block.scalar
        def _(act):
            af = nc.scalar.activation
            chain = Chain(act, s_ac)

            def split_hi(n, p, slot):
                act.wait_ge(s_raw[slot], n.half().half().value(16, 16))
                nc.scalar.copy(w_hi[p][:], raw[:, slot, :, p * P:(p + 1) * P]).then_inc(s_hi, 1)

            def step(n, more=True):
                act.wait_ge(s_done, n.value(1, 1))
                if more:
                    c = n.base % 4
                    split_hi(n + 2, c % 2, ((c + 2) // 2) % 2)

            def ada_split(m):
                if m.i is not None or m.base >= 2:
                    act.wait_ge(s_ad, m.value(add=-1))
                src, s_loaded, v = ada_slot(m)
                act.wait_ge(s_loaded, v)
                nc.scalar.copy(wa[m.base % 2][:, 0], src).then_inc(s_wah, 1)

            def ada_rows(m):
                slot = m.base % 2
                if m.i is not None or m.base >= 2:
                    act.wait_ge(s_at, m.value(add=-1))
                act.wait_ge(s_ad, m.value(1, 1))
                nc.scalar.copy(rows_a[:, slot], pg[0:20, 2 + slot, 0:256]).then_inc(s_ar, 1)

            def psum(p):
                return pu[p][:, :, 0:HALF]

            def square(q, t, src, s=None, v=0):
                if t.i is not None or t.base >= 2:
                    act.wait_ge(s_sqf, t.value(add=KT * q - 1))
                if s is not None:
                    act.wait_ge(s, t.value(add=v + 1))
                af(sg[:, t.base % 2, :], tile(src, t.value()), ACT.Square).then_inc(s_sq, 1)

            def rstd(ss):
                act.wait_ge(s_ss, ss)
                chain.link(af(halves(sg[:, 3, :]), pg[:, 0:2, 0:HALF], ACT.Ln, scale=1 / D, bias=eps[:]))
                af(sg[:, 3, :], sg[:, 3, :], ACT.Exp, scale=-0.5).then_inc(s_root, 1)

            def modulate(j, sc, sh):
                for t in range(KT):
                    act.wait_ge(s_xn, KT * j + t + 1)
                    full = sg[:, t % 2, 0:NP]
                    af(full, full, ACT.Identity, bias=mod[:, 8 * sh + t, 0:1], scale=mod[:, 8 * sc + t, 0:1]
                       ).then_inc(s_hf, 1)
                    act.wait_ge(s_hf, KT * j + t + 1)
                    nc.scalar.copy(h_hi[:, t, 0:NP], full).then_inc(s_hh, 1)

            act.dma_start(crow[0:1, :], A["c_prompt"]).then_inc(s_ld["c"], 16)
            act.dma_start(crow[1:9, :], A["c_sample"]).then_inc(s_ld["c"], 16)
            xp = A["x_prompt"][0].rearrange("(c p) d -> c p d", p=P)
            for c in range(4):
                act.dma_start(xtok[:, c, :], xp[c]).then_inc(s_ld["x"], 16)
            act.dma_start(xsrow, A["x_sample"].rearrange("b t d -> (b t) d")).then_inc(s_ld["xs"], 16)
            for name in VECS:
                v = A[name] if name == "norm_final" else A[name][0]
                r = v.shape[0] // P
                act.dma_start(vrow[VROW[name]:VROW[name] + r, :], v.rearrange("(r n) -> r n", n=P)
                              ).then_inc(s_ld["vec"], 16)
            act.dma_start(brow[0:72, :], A["b_ada"][0].rearrange("(r n) -> r n", n=P)).then_inc(s_ld["b"], 16)
            act.dma_start(brow[72:88, :], A["b_ada_final"].rearrange("(r n) -> r n", n=P)).then_inc(s_ld["b"], 16)
            cwr = A["conv_w"][0].rearrange("j (t n) -> (j t) n", n=P)
            for g in range(2):
                act.dma_start(cwrow[:, g, :], cwr[g * 124:(g + 1) * 124, :]).then_inc(s_ld["cw"], 16)

            act.wait_ge(s_td, 1)
            act.wait_ge(s_tp, 1)
            af(c_f[:, :, 0:9], pg[:, 0, 0:80].rearrange("p (t n) -> p t n", n=10)[:, :, 0:9], ACT.Silu
               ).then_inc(s_te, 1)
            act.wait_ge(s_te, 1)
            nc.scalar.copy(c_hl[:, :, 0:10], c_f[:]).then_inc(s_c, 1)
            for t in range(KT):
                act.wait_ge(s_tp, 3 + t)
                nc.scalar.copy(x[:, t, 0:NP], pg[:, 2 + t % 2, :]).then_inc(s_te, 1)
            act.wait_ge(s_tp, 2 + KT)
            act.wait_ge(s_te, 1 + KT)
            act.wait_ge(s_td, 1 + KT)
            for t in range(KT):
                square(0, Lin(t), x)
            for m in range(2):
                ada_split(Lin(m))
            rstd(1)
            for m in range(ADA0):
                ada_rows(Lin(m))
                ada_split(Lin(m + 2))
            for n in range(2):
                split_hi(Lin(n), n, 0)
            modulate(0, SC1, SH1)

            def ffn(which):
                def ada_part(c, m, i, last=False):
                    if which == 1 and c % 2 == 0:
                        ada_rows(Lin(m + c // 2, 2, i))
                        if not last:
                            ada_split(Lin(m + c // 2 + 2, 2, i))

                for g in range(3):
                    n0 = at[f"up{which}_{g}"]
                    a0 = (which - 1) * (FF // P) + sum(GROUPS[:g])
                    for i, k0 in bodies(act, GROUPS[g] // 2, n0 == 0):
                        for c in range(4):
                            n = Lin(n0 + 4 * k0 + c, 4, i)
                            hidden = lambda add: Lin(a0 + 2 * k0 + add, 2, i).value()
                            step(n)
                            if c < 2:
                                act.wait_ge(s_a, hidden(HIDDEN0))
                                af(halves(sg[:, c, :]), psum(c), ACT.Silu).then_inc(s_evac[c], 1)
                            else:
                                act.wait_ge(s_evac[c % 2], n.half().value(1, 1))
                                nc.scalar.copy(tile(f_hi, Lin(2 * k0 + c - 2, 2, i).value()), sg[:, c - 2, :]
                                               ).then_inc(s_ahi, 1)
                            ada_part(c, ADA_UP[g] + 2 * k0, i)
                    n0 = at[f"down{which}_{g}"]
                    if g == 2:
                        for c in range(8):
                            step(Lin(n0 + c), n0 + c + 2 < UNITS)
                            ada_part(c, ADA_DOWN[g], None, last=c // 4 == 1)
                            square((1, 4)[which - 1], Lin(c), x, s_x, (2, 6)[which - 1] * KT)
                    else:
                        with act.Fori(0, 2) as i:
                            for c in range(4):
                                step(Lin(n0 + c, 4, i))
                                ada_part(c, ADA_DOWN[g], i)

            ffn(1)
            rstd(2)
            modulate(1, SC2, SH2)
            for t in range(KT):
                act.wait_ge(s_cvt, t + 1)
                nc.scalar.copy(sT[:, t, :, 0:TAPS - 1],
                               pg[:, t % 4, 0:240].rearrange("p (b j) -> p b j", b=NS)).then_inc(s_cve, 1)

            def conv_units(i, n0, per):
                for c in range(4):
                    n = Lin(n0 + c, per, i)
                    step(n)
                    if c < 2:
                        if i is not None:
                            act.wait_ge(s_evac[c], n.half().value())
                        af(halves(sg[:, c, :]), psum(c), ACT.Sigmoid).then_inc(s_evac[c], 1)

            conv_units(None, at["conv"], 0)
            with act.Fori(0, 3) as i:
                conv_units(i, at["conv"] + 4, 4)
            n = at["alr"]
            act.wait_ge(s_done, n + 1)
            for e in (1, 0):
                nc.scalar.copy(alr[:, e * HALF:(e + 1) * HALF], pu[0][0:RANK, e, 0:HALF]).then_inc(s_evac[e], 2)
            for c in range(4):
                if c >= 2:
                    act.wait_ge(s_lo, n + c + 1)
                step(Lin(n + c))
            act.wait_ge(s_ct, 1)
            nc.scalar.copy(flat(sg[:])[0:38, 0:D].rearrange("p (e n) -> p e n", e=2), pg[0:38, 0:2, :]
                           ).then_inc(s_cts, 1)
            for h in range(HEADS):
                act.wait_ge(s_lg, h + 1)
                b = 2 * (h % 2)
                af(halves(lb[:, h, :]), pg[:, b:b + 2, 0:HALF], ACT.Identity,
                   bias=vt[:, VROW["b_alpha"] + h:VROW["b_alpha"] + h + 1]).then_inc(s_z, 1)
            for h in range(HEADS):
                act.wait_ge(s_az, h + 1)
                w = sg[:, 2 + h % 2, :]
                chain.link(af(w, w, ACT.Exp, scale=-1.0))
                af(w, w, ACT.Ln, bias=ones[:, 0:1]).then_inc(s_l, 1)
            with act.Fori(0, 2) as i:
                for c in range(4):
                    step(Lin(at["qk"] + c, 4, i))
                    af(halves(tile(qk, i + 2 * c)), psum(c % 2), ACT.Copy,
                       scale=qk_scale[:, bass.ds(i, 1)]).then_inc(s_evac[c % 2], 1)
            act.wait_ge(s_cst, 32)
            act.wait_ge(s_b, HEADS)
            act.wait_ge(s_cvs, 1)
            act.wait_ge(s_xsp, 16)
            with act.Fori(0, 2) as i:
                for c in range(4):
                    step(Lin(at["v"] + c, 4, i))
                    nc.scalar.copy(halves(sg[:, c, :]), psum(c % 2)).then_inc(s_evac[c % 2], 1)
                for e in range(2):
                    act.wait_ge(s_vt, i * 2 + (e + 1))
                    f = i * 512 + 256 * e
                    nc.scalar.copy(vtok[:, :, bass.ds(f, DV)],
                                   pg[:, 0:2, :].rearrange("p a (c n) -> p (a c) n", c=2))
                    nc.scalar.copy(vs[:, bass.ds(f, DV)], pg[0:NS, 2, 0:DV]).then_inc(s_v, 1)

            def gate(i, c):
                n = Lin(at["gates"] + c, 12, i)
                p, j = c % 2, c % 4
                step(n)
                if c >= 4:
                    act.wait_ge(s_gsp[j], i * 48 + 16 * (c // 4))
                t = af(halves(sg[:, j, :]), psum(p), ACT.Tanh, scale=0.5)
                t.then_inc(s_gt if c < 4 else s_evac[p], 1)
                act.wait_ge(s_evac[p], n.half().value(1, 1))
                act.dma_start(gates_d[c // 4][bass.ds(i * 4 + j, 1)].rearrange("o p n -> (o p) n"), sg[:, j, :]
                              ).then_inc(s_gsp[j], 16)

            def exp(h, l):
                act.wait_ge(s_gd, h.value(8, l + 2))
                af(E_[:, l % 2, :], E_[:, l % 2, :], ACT.Exp, scale=1 / 16).then_inc(s_ge, 1)

            with act.Fori(0, 2) as i:
                for hh in range(2):
                    h = Lin(hh, 2, i)
                    for s in range(6):
                        gate(i, 6 * hh + s)
                        if s == 0:
                            af(EB, tile(lb, h.value()), ACT.Exp, scale=1 / 16).then_inc(s_ge, 1)
                            act.wait_ge(s_gd, h.value(8, 1))
                            af(E_[:, 0, :], E_[:, 0, :], ACT.Exp, scale=1 / 16).then_inc(s_ge, 1)
                            nc.scalar.copy(VH, vtok[:, :, bass.ds(h.value(DV), DV)]).then_inc(s_gk, 1)
                            exp(h, 0)
                            exp(h, 1)
                        if s == 1:
                            act.wait_ge(s_kt, h.value(1, 1))
                            nc.scalar.copy(KTK, pg[:, 2, :].rearrange("p (c n) -> p c n", c=NC)).then_inc(s_kr, 1)
                            nc.scalar.copy(ks8[:], pg[0:NS, 3, 0:DK]).then_inc(s_kr, 1)
                            exp(h, 2)
                            exp(h, 3)
                        if s == 2:
                            exp(h, 4)
                            exp(h, 5)
                        if s == 3:
                            exp(h, 6)
                        if s == 5:
                            dst = qk[:, bass.ds(h.value(2), 2), :]
                            act.wait_ge(s_o, h.value(2, 1))
                            nc.scalar.copy(dst[:, :, NP:N], pg[:, 2, 0:2 * NS].rearrange("p (t b) -> p t b", t=2)
                                           ).then_inc(s_oe, 1)
                            act.wait_ge(s_o, h.value(2, 2))
                            nc.scalar.copy(dst[:, :, 0:NP], pg[:, 2:4, :]).then_inc(s_oe, 1)
                for j in range(4):
                    act.wait_ge(s_gsp[j], i * 48 + 48)

            for t in range(KT):
                square(2, Lin(t), d, s_cen)
            rstd(4)
            for t in range(KT):
                act.wait_ge(s_xn, 2 * KT + t + 1)
                af(d[:, t, :], d[:, t, :], ACT.Silu, scale=vt[:, VROW["conv_ln_g"] + t:VROW["conv_ln_g"] + t + 1],
                   bias=vt[:, VROW["conv_ln_b"] + t:VROW["conv_ln_b"] + t + 1]).then_inc(s_hf, 1)
                act.wait_ge(s_hf, 2 * KT + t + 1)
                nc.scalar.copy(h_hi[:, t, :], d[:, t, :]).then_inc(s_hh, 1)
            act.wait_ge(s_oe, 2 * HEADS)
            for h in range(HEADS):
                if h:
                    act.wait_ge(s_osum, h)
                af(flat(sg[:])[:, 0:2 * N], qk[:, 2 * h:2 * h + 2, :].rearrange("p a n -> p (a n)"), ACT.Square
                   ).then_inc(s_osq, 1)
            for h in range(HEADS):
                b = 2 * (h % 2)
                act.wait_ge(s_os, h + 1)
                chain.link(af(halves(lb[:, h, :]), pg[:, b:b + 2, 0:HALF], ACT.Ln, scale=1 / DV, bias=eps[:]))
                af(lb[:, h, :], lb[:, h, :], ACT.Exp, scale=-0.5).then_inc(s_om, 1)
            with act.Fori(0, 2) as i:
                for c in range(4):
                    step(Lin(at["yconv"] + c, 4, i))
                    act.wait_ge(s_of, i * 4 + (c + 1))
                    nc.scalar.copy(tile(o_hi, i * 4 + c), tile(qk, i * 4 + c)).then_inc(s_oh, 1)
            with act.Fori(0, 2) as i:
                for c in range(4):
                    step(Lin(at["ygla"] + c, 4, i))
                    act.wait_ge(s_mf, i * 4 + (c + 1))
                    nc.scalar.copy(tile(h_hi, i * 4 + c), sg[:, c % 2, :]).then_inc(s_mh, 1)
            for i, k in bodies(act, 2, 1):
                for c in range(4):
                    step(Lin(at["out"] + 4 * k + c, 4, i))
                    square(3, Lin(4 * k + c, 4, i), x, s_x, 3 * KT)
            rstd(5)
            modulate(3, SC3, SH3)
            ffn(2)
            rstd(6)
            for t in range(KT):
                act.wait_ge(s_xn, 4 * KT + t + 1)
                af(x[:, t, 0:NP], sg[:, t % 2, 0:NP], ACT.Identity, bias=mod[:, 8 * SHF + t, 0:1],
                   scale=mod[:, 8 * SCF + t, 0:1]).then_inc(s_yn, 1)
            act.wait_ge(s_yt, 1)
            nc.scalar.copy(ysrow.rearrange("p (e n) -> p e n", e=2), pu[0][0:NS, :, :]).then_inc(s_yse, 1)

        @block.vector
        def _(dve):
            V = nc.vector
            chain = Chain(dve, s_dv)
            conv = Chain(dve, s_cv)

            def split_lo(n, p, slot):
                dve.wait_ge(s_raw[slot], n.half().half().value(16, 16))
                dve.wait_ge(s_hi, n.value(1, 1))
                V.tensor_tensor(w_lo[p][:], raw[:, slot, :, p * P:(p + 1) * P], w_hi[p][:].bitcast(F32),
                                ALU.subtract).then_inc(s_lo, 1)

            def step(n, more=True):
                dve.wait_ge(s_done, n.value(1, 1))
                if more:
                    c = n.base % 4
                    split_lo(n + 2, c % 2, ((c + 2) // 2) % 2)

            def psum(p):
                return pu[p][:, :, 0:HALF]

            def part(j):
                return mod[:, 8 * j:8 * j + 8, :]

            def vec(r):
                return vt[:, r:r + KT].unsqueeze(2).to_broadcast([P, KT, 10])

            def ada_split(m):
                slot = m.base % 2
                dve.wait_ge(s_wah, m.value(1, 1))
                V.tensor_tensor(wa[slot][:, 1], ada_slot(m)[0], wa[slot][:, 0].bitcast(F32), ALU.subtract
                                ).then_inc(s_wal, 1)

            def ada_out(m):
                dve.wait_ge(s_at, m.value(1, 1))
                bias = vt[:, bass.ds(m.value(2, NVEC), 2)].unsqueeze(2).to_broadcast([P, 2, 10])
                V.tensor_tensor(mod[:, bass.ds(m.value(2), 2), :],
                                pg[:, m.base % 2, 0:20].rearrange("p (t c) -> p t c", t=2), bias, ALU.add
                                ).then_inc(s_mod, 1)

            def scale_of(j, gain):
                dve.wait_ge(s_mod, 4 * j + 4)
                chain.link(V.scalar_tensor_tensor(part(j), part(j), 1.0, vec(VROW[gain]), ALU.add, ALU.mult))

            def gate_of(j):
                dve.wait_ge(s_mod, 4 * j + 4)
                chain.link(V.tensor_scalar(part(j), part(j), 0.5, None, ALU.mult))

            def add_square(q, t):
                dve.wait_ge(s_sq, t.value(add=KT * q + 1))
                if t.i is None and t.base == 0:
                    V.tensor_copy(sg[:, 2, :], sg[:, 0, :]).then_inc(s_sqf, 1)
                else:
                    dve.wait_ge(s_sqf, t.value(add=KT * q))
                    V.tensor_tensor(sg[:, 2, :], sg[:, 2, :], sg[:, t.base % 2, :], ALU.add).then_inc(s_sqf, 1)

            def refine(r, ps, n):
                w = sg[:, 2, :]
                chain.link(V.tensor_tensor(w, r, r, ALU.mult))
                chain.link(V.scalar_tensor_tensor(halves(w), ps, n * EPS, halves(w), ALU.add, ALU.mult))
                chain.link(V.tensor_scalar(w, w, -0.5 / n, 1.5, ALU.mult, ALU.add))
                return V.tensor_tensor(r, r, w, ALU.mult)

            def rstd(j):
                dve.wait_ge(s_root, j)
                refine(sg[:, 3, :], pg[:, 0:2, 0:HALF], D).then_inc(s_rstd, 1)

            def modulate(j, sc, sh, final=False):
                if j:
                    rstd(j + 1)
                dve.wait_ge(s_rstd, j + 1)

                def samples():
                    rs = sg[:, 3, NP:N].unsqueeze(1).to_broadcast([P, KT, NS])
                    chain.link(V.tensor_tensor(hs[:], x[:, :, NP:N], rs, ALU.mult))
                    chain.link(V.tensor_tensor(hs[:], hs[:], part(sc)[:, :, 1:9], ALU.mult))
                    if final:
                        V.tensor_tensor(x[:, :, NP:N], hs[:], part(sh)[:, :, 1:9], ALU.add).then_inc(s_ys, 1)
                    else:
                        chain.link(V.tensor_tensor(hs[:], hs[:], part(sh)[:, :, 1:9], ALU.add))
                        chain.link(V.tensor_copy(h_hi[:, :, NP:N], hs[:]))
                        V.tensor_tensor(h_lo[:, :, NP:N], hs[:], h_hi[:, :, NP:N].bitcast(F32), ALU.subtract)

                def normed(t):
                    if final and t >= 2:
                        dve.wait_ge(s_yn, t - 1)
                    if not final and t >= 2:
                        dve.wait_ge(s_h, KT * j + t - 1)
                    V.tensor_tensor(sg[:, t % 2, 0:NP], x[:, t, 0:NP], sg[:, 3, 0:NP], ALU.mult).then_inc(s_xn, 1)

                def staged(t):
                    dve.wait_ge(s_yt, t + 2)
                    V.tensor_copy(ytok[:, :, t * P:(t + 1) * P], pg[:, t % 4, :].rearrange("p (c n) -> p c n", c=4)
                                  ).then_inc(s_ye, 1)

                normed(0)
                for t in range(KT):
                    if t + 1 < KT:
                        normed(t + 1)
                    if t == 0:
                        samples()
                    if final:
                        staged(t)
                    if not final:
                        dve.wait_ge(s_hh, KT * j + t + 1)
                        V.tensor_tensor(h_lo[:, t, 0:NP], sg[:, t % 2, 0:NP], h_hi[:, t, 0:NP].bitcast(F32),
                                        ALU.subtract).then_inc(s_h, 1)

            def residual(n, m, gt):
                p = n.base % 2
                g = lambda a, b: flat(mod[:, bass.ds(m + 8 * gt, 1), a:b])
                ps = pu[p]
                V.scalar_tensor_tensor(tile(x, m, 0, HALF), ps[:, 0, 0:HALF], g(0, 1), tile(x, m, 0, HALF),
                                       ALU.mult, ALU.add)
                V.scalar_tensor_tensor(tile(x, m, HALF, NP), ps[:, 1, 0:NP - HALF], g(0, 1), tile(x, m, HALF, NP),
                                       ALU.mult, ALU.add)
                V.tensor_tensor(t8[:, p, :], ps[:, 1, NP - HALF:HALF], g(1, 9), ALU.mult).then_inc(s_evac[p], 1)
                dve.wait_ge(s_evac[p], n.half().value(1, 1))
                V.tensor_tensor(tile(x, m, NP, N), tile(x, m, NP, N), t8[:, p, :], ALU.add).then_inc(s_x, 1)

            V.memset(c_f[:], 0.0).then_inc(s_cf, 1)
            V.memset(t8[:], 0.0).then_inc(s_a, HIDDEN0)
            dve.wait_ge(s_cf, 1)
            dve.wait_ge(s_tp, 2)
            V.tensor_copy(vt[:], pg[:, 1, 0:NVEC + NADA])
            V.tensor_copy(cw[:], pg[:, 1, 160:160 + TAPS * KT]).then_inc(s_td, 1)
            dve.wait_ge(s_c, 1)
            V.tensor_tensor(c_hl[:, :, 10:20], c_f[:], c_hl[:, :, 0:10].bitcast(F32), ALU.subtract).then_inc(s_c, 1)
            for t in range(KT):
                dve.wait_ge(s_tp, 3 + t)
                V.tensor_copy(x[:, t, NP:N], pg[:, t % 2, 0:NS]).then_inc(s_td, 1)
            for t in range(KT):
                add_square(0, Lin(t))
            for m in range(2):
                ada_split(Lin(m))
            rstd(1)
            for m in range(ADA0):
                ada_out(Lin(m))
                ada_split(Lin(m + 2))
            for n in range(2):
                split_lo(Lin(n), n, 0)
            scale_of(SC1, "norm_ffn1")
            modulate(0, SC1, SH1)

            def ffn(which, gt):
                def ada_part(c, m, i, last=False):
                    if which == 1 and c % 2:
                        ada_out(Lin(m + c // 2, 2, i))
                    elif which == 1 and not last:
                        ada_split(Lin(m + c // 2 + 2, 2, i))

                a0 = (which - 1) * (FF // P)
                for g in range(3):
                    n0 = at[f"up{which}_{g}"]
                    a1 = a0 + sum(GROUPS[:g])
                    for i, k0 in bodies(dve, GROUPS[g] // 2, n0 == 0):
                        for c in range(4):
                            n = Lin(n0 + 4 * k0 + c, 4, i)
                            step(n)
                            if c >= 2:
                                p = c % 2
                                s = sg[:, p, :]
                                dve.wait_ge(s_evac[p], (n + (-2)).half().value(1, 1))
                                V.tensor_tensor(halves(s), halves(s), psum(p), ALU.mult).then_inc(s_evac[p], 1)
                                t = Lin(2 * k0 + p, 2, i)
                                dve.wait_ge(s_ahi, t.value(add=a1 + 1))
                                V.tensor_tensor(tile(f_lo, t.value()), s, tile(f_hi, t.value()).bitcast(F32),
                                                ALU.subtract).then_inc(s_a, 1)
                            ada_part(c, ADA_UP[g] + 2 * k0, i)
                    if g == 0:
                        gate_of(gt)
                    n0 = at[f"down{which}_{g}"]
                    if g == 2:
                        q = (1, 4)[which - 1]
                        for c in range(8):
                            step(Lin(n0 + c), n0 + c + 2 < UNITS)
                            residual(Lin(n0 + c), c, gt)
                            if c:
                                add_square(q, Lin(c - 1))
                            ada_part(c, ADA_DOWN[g], None, last=c // 4 == 1)
                        add_square(q, Lin(KT - 1))
                    else:
                        with dve.Fori(0, 2) as i:
                            for c in range(4):
                                n = Lin(n0 + c, 4, i)
                                step(n)
                                residual(n, i * 4 + c, gt)
                                ada_part(c, ADA_DOWN[g], i)

            ffn(1, GT1)
            scale_of(SC2, "norm_mix")
            gate_of(GT2)
            modulate(1, SC2, SH2)
            chain.link(V.memset(u[:, :, 0:TAPS - 1], 0.0))
            V.memset(SC, 0.0)

            def conv_first(pair):
                for t in (2 * pair, 2 * pair + 1):
                    conv.mark(V.tensor_scalar(d[:, t, 0:NP], u[:, t, 0:NP], cw[:, t:t + 1],
                                              vt[:, VROW["conv_b"] + t:VROW["conv_b"] + t + 1], ALU.mult, ALU.add))

            def conv_taps(pair, tap, count):
                for s in range(count):
                    for t in (2 * pair, 2 * pair + 1):
                        conv.wait(back=1)
                        conv.mark(V.scalar_tensor_tensor(
                            d[:, t, 0:NP], flat(u[:, t:t + 1, bass.ds(tap + s, NP)]),
                            cw[:, bass.ds((tap + s) * KT + t, 1)], d[:, t, 0:NP], ALU.mult, ALU.add))

            def conv_units(i, n0, per, t0, taps=False):
                for c in range(4):
                    n = Lin(n0 + c, per, i)
                    step(n)
                    if c >= 2:
                        p = c % 2
                        dve.wait_ge(s_evac[p], (n + (-2)).half().value(1, 1))
                        V.tensor_tensor(halves(tile(u, t0 + p, TAPS - 1, UP)), halves(sg[:, p, :]), psum(p),
                                        ALU.mult).then_inc(s_evac[p], 1)
                    if taps:
                        conv_taps(0, i * 10 + (1 + (0, 3, 6, 8)[c]), (3, 3, 2, 2)[c])

            conv_units(None, at["conv"], 0, 0)
            for p in range(2):
                dve.wait_ge(s_evac[p], (at["conv"] + 2) // 2 + 1)
            conv_first(0)
            with dve.Fori(0, 3) as i:
                conv.loop(i, 20)
                conv_units(i, at["conv"] + 4, 4, i * 2 + 2, taps=True)
            conv.end(3)
            n = at["alr"]
            for c in range(4):
                if c >= 2:
                    dve.wait_ge(s_lo, n + c + 1)
                step(Lin(n + c))
            dve.wait_ge(s_evac[0], n // 2)
            dve.wait_ge(s_evac[1], n // 2)
            dve.wait_ge(s_cve, KT)
            chain.link(V.tensor_copy(sT[:, :, :, TAPS - 1], u[:, :, UP - NS:UP]))
            taps = cw[:].rearrange("p (j t) -> p t j", t=KT)
            for t in range(KT):
                chain.mark(V.tensor_tensor(sT[:, t], sT[:, t], taps[:, t:t + 1, :].to_broadcast([P, NS, TAPS]), ALU.mult))
            chain.wait()
            for t in range(KT):
                chain.mark(V.tensor_reduce(d[:, t, NP:N], sT[:, t], AX_X, ALU.add))
            chain.wait()
            V.tensor_tensor(d[:, :, NP:N], d[:, :, NP:N],
                            vt[:, VROW["conv_b"]:VROW["conv_b"] + KT].unsqueeze(2).to_broadcast([P, KT, NS]),
                            ALU.add).then_inc(s_cvs, 1)
            for h in range(HEADS):
                dve.wait_ge(s_z, h + 1)
                z, w = lb[:, h, :], sg[:, 2 + h % 2, :]
                if h < 2:
                    V.scalar_tensor_tensor(w, z, -1.0, z, ALU.mult, ALU.max).then_inc(s_az, 1)
            for h in range(HEADS):
                z, w = lb[:, h, :], sg[:, 2 + h % 2, :]
                dve.wait_ge(s_l, h + 1)
                chain.link(V.scalar_tensor_tensor(z, z, 0.0, w, ALU.min, ALU.subtract))
                for c in range(NC):
                    v = lb[:, h, c * CH:(c + 1) * CH]
                    last = V.tensor_tensor_scan(v, ones[:], v, 0.0, ALU.mult, ALU.add)
                last.then_inc(s_b, 1)
                if h + 2 < HEADS:
                    z2 = lb[:, h + 2, :]
                    V.scalar_tensor_tensor(w, z2, -1.0, z2, ALU.mult, ALU.max).then_inc(s_az, 1)
            conv_first(1)
            with dve.Fori(0, 2) as i:
                conv.loop(i, 30)
                for c in range(4):
                    step(Lin(at["qk"] + c, 4, i))
                    conv_taps(1, i * 15 + (1 + 4 * c), 4 if c < 3 else 3)
            conv.end(2)
            conv_first(2)
            with dve.Fori(0, 2) as i:
                conv.loop(i, 30)
                for c in range(4):
                    step(Lin(at["v"] + c, 4, i))
                    conv_taps(2, i * 15 + (1 + 4 * c), 4 if c < 3 else 3)
            conv.end(2)
            conv_first(3)

            def diff(h, l):
                w = LEVELS[l]
                blocks = lambda v: v.rearrange("p (b e t) -> p b e t", e=2, t=w)
                b, e = blocks(tile(lb, h.value(), 0, NP)), blocks(E_[:, l % 2, :])
                dve.wait_ge(s_gm, h.value(10, MIX[l - 2] if l >= 2 else MIX["k"]))
                mid = b[:, :, 0, w - 1:w].to_broadcast([P, NP // (2 * w), w])
                V.tensor_tensor(e[:, :, 1, :], b[:, :, 1, :], mid, ALU.subtract)
                V.tensor_tensor(e[:, :, 0, :], mid, b[:, :, 0, :], ALU.subtract).then_inc(s_gd, 1)

            def mix(h, l):
                w = LEVELS[l]
                blocks = lambda v: v.rearrange("p (b e t) -> p b e t", e=2, t=w)
                dve.wait_ge(s_ge, h.value(9, l + 3))
                if l >= 2:
                    dve.wait_ge(s_gg, h.value(8, l - 1))
                e, m = blocks(E_[:, l % 2, :]), blocks(M_[:, l % 2, 0:NP])
                q, k = (blocks(tile(qk, h.value(2, j), 0, NP)) for j in (0, 1))
                V.tensor_tensor(m[:, :, 1, :], e[:, :, 1, :], q[:, :, 1, :], ALU.mult)
                V.tensor_tensor(m[:, :, 0, :], e[:, :, 0, :], k[:, :, 0, :], ALU.mult).then_inc(s_gm, 1)

            def merge(h, l):
                if l:
                    dve.wait_ge(s_gp, h.value(8, l))
                    dve.sem_inc(s_merge, 1)
                V.copy_predicated(SC.rearrange("p (c t) -> p c t", c=NC),
                                  masks[:, l:l + 1, :].bitcast(U16).to_broadcast([P, NC, CH]),
                                  pg[:, l % 2, :].rearrange("p (c t) -> p c t", c=NC)).then_inc(s_gp, 1)

            def sample_states(h, r):
                dve.wait_ge(s_ko, h.value(2, r + 1))
                for b in range(4):
                    j = 4 * r + b
                    V.scalar_tensor_tensor(ST[:, j, :], ST[:, j, :], EB[:, NP + j:NP + j + 1],
                                           pg[:, 2 + b // 2, (b % 2) * DV:(b % 2 + 1) * DV],
                                           ALU.mult, ALU.add).then_inc(s_sn, 1)

            with dve.Fori(0, 2) as i:
                conv.loop(i, 30)
                for hh in range(2):
                    h = Lin(hh, 2, i)
                    for s in range(6):
                        c = 6 * hh + s
                        n = Lin(at["gates"] + c, 12, i)
                        step(n)
                        if c < 4:
                            dve.wait_ge(s_gt, i * 4 + (c + 1))
                            V.scalar_tensor_tensor(halves(sg[:, c, :]), halves(sg[:, c, :]), 1.0, psum(c % 2),
                                                   ALU.add, ALU.mult).then_inc(s_evac[c % 2], 1)
                        if s == 0:
                            b = tile(lb, h.value(), 0, NP).rearrange("p (c t) -> p c t", c=NC)
                            end = b[:, :, CH - 1:CH].to_broadcast([P, NC, CH])
                            V.tensor_tensor(E_[:, 0, :].rearrange("p (c t) -> p c t", c=NC), end, b,
                                            ALU.subtract).then_inc(s_gd, 1)
                            dve.wait_ge(s_ge, h.value(9, 2))
                            V.tensor_copy(M_[:, 0, NP:N], tile(qk, h.value(2, 1), NP, N))
                            V.tensor_tensor(M_[:, 0, 0:NP], E_[:, 0, :], tile(qk, h.value(2, 1), 0, NP),
                                            ALU.mult).then_inc(s_gm, 1)
                            diff(h, 0)
                            diff(h, 1)
                        if s == 1:
                            dve.wait_ge(s_kt, h.value(1, 1))
                            V.tensor_tensor(QS, EB[:, 0:NP], tile(qk, h.value(2), 0, NP), ALU.mult).then_inc(s_gm, 1)
                            mix(h, 0)
                            diff(h, 2)
                            mix(h, 1)
                            diff(h, 3)
                            dve.wait_ge(s_kr, h.value(2, 2))
                            V.tensor_tensor(km, ks8[:].unsqueeze(1).to_broadcast([NS, NS, DK]),
                                            ident[0:NS, 0:NS].unsqueeze(2).to_broadcast([NS, NS, DK]),
                                            ALU.mult).then_inc(s_km, 1)
                        if s == 2:
                            dve.wait_ge(s_ds, h.value(1, 1))
                            dve.wait_ge(s_st, h.value(16, 16))
                            V.tensor_copy(SB[:, 0, :], pg[:, 2, 0:DV]).then_inc(s_S, 1)
                            for k in range(1, NC):
                                dve.wait_ge(s_S, h.value(4, k))
                                V.scalar_tensor_tensor(SB[:, k, :], SB[:, k - 1, :], EB[:, k * CH + CH - 1:(k + 1) * CH],
                                                       pg[:, 2 + k // 2, (k % 2) * DV:(k % 2 + 1) * DV],
                                                       ALU.mult, ALU.add).then_inc(s_S, 1)
                            mix(h, 2)
                            merge(h, 0)
                            diff(h, 4)
                            mix(h, 3)
                            merge(h, 1)
                            diff(h, 5)
                        if s == 3:
                            sample_states(h, 0)
                            mix(h, 4)
                            merge(h, 2)
                            diff(h, 6)
                            mix(h, 5)
                            merge(h, 3)
                        if s == 4:
                            sample_states(h, 1)
                            mix(h, 6)
                            merge(h, 4)
                            dve.wait_ge(s_gg, h.value(8, 6))
                            V.tensor_scalar(M_[:, 1, 0:NP], tile(qk, h.value(2, 1), 0, NP), 1.0, None, ALU.mult
                                            ).then_inc(s_gm, 1)
                            merge(h, 5)
                        done, more = (15 * c) // 12, (15 * (c + 1)) // 12
                        if s == 5:
                            dve.wait_ge(s_gg, h.value(8, 8))
                        conv_taps(3, i * 15 + (1 + done), more - done)
                        if s == 5:
                            merge(h, 6)
                            merge(h, 7)
            conv.end(2)

            conv.wait()
            dve.wait_ge(s_gsp[2], 6 * 16)
            dve.wait_ge(s_gsp[3], 6 * 16)
            for t in range(KT):
                if t == 0:
                    V.tensor_copy(sg[:, 2, :], d[:, 0, :]).then_inc(s_ln, 1)
                else:
                    dve.wait_ge(s_ln, t)
                    V.tensor_tensor(sg[:, 2, :], sg[:, 2, :], d[:, t, :], ALU.add).then_inc(s_ln, 1)
            dve.wait_ge(s_ss, 3)
            chain.link(V.tensor_scalar(halves(sg[:, 3, :]), pg[:, 0:2, 0:HALF], 1 / D, None, ALU.mult))
            for t in range(KT):
                V.tensor_tensor(d[:, t, :], d[:, t, :], sg[:, 3, :], ALU.subtract).then_inc(s_cen, 1)
            for t in range(KT):
                add_square(2, Lin(t))
            rstd(3)
            dve.wait_ge(s_rstd, 3)
            for t in range(KT):
                V.tensor_tensor(d[:, t, :], d[:, t, :], sg[:, 3, :], ALU.mult).then_inc(s_xn, 1)
            for t in range(KT):
                dve.wait_ge(s_hh, 2 * KT + t + 1)
                V.tensor_tensor(h_lo[:, t, :], d[:, t, :], h_hi[:, t, :].bitcast(F32), ALU.subtract).then_inc(s_h, 1)
            for h in range(HEADS):
                dve.wait_ge(s_osq, h + 1)
                V.tensor_tensor(lb[:, h, :], sg[:, 0, :], sg[:, 1, :], ALU.add).then_inc(s_osum, 1)
            for h in range(HEADS):
                b = 2 * (h % 2)
                dve.wait_ge(s_om, h + 1)
                if h:
                    dve.wait_ge(s_or, h)
                refine(lb[:, h, :], pg[:, b:b + 2, 0:HALF], DV).then_inc(s_or, 1)
            gn = vt[:, VROW["gla_norm"]:VROW["gla_norm"] + KT]
            chain.link(V.tensor_scalar(gn, gn, 0.5, None, ALU.mult))
            dve.wait_ge(s_or, HEADS)
            dve.wait_ge(s_gr["r"], 16)
            dve.wait_ge(s_gr["gc"], 16)
            with dve.Fori(0, 2) as i:
                for c in range(4):
                    n = Lin(at["yconv"] + c, 4, i)
                    t = i * 4 + c
                    step(n)
                    V.scalar_tensor_tensor(halves(tile(work_t, t + KT)), halves(tile(work_t, t + KT)), 1.0, psum(c % 2),
                                           ALU.add, ALU.mult).then_inc(s_evac[c % 2], 1)
                    ot = tile(qk, t)
                    V.tensor_tensor(ot, ot, tile(lb, i * 2 + c // 2), ALU.mult).then_inc(s_ox, 1)
                    dve.wait_ge(s_ox, i * 4 + (c + 1))
                    V.scalar_tensor_tensor(ot, ot, vt[:, bass.ds(t + VROW["gla_norm"], 1)], tile(d, t),
                                           ALU.mult, ALU.mult).then_inc(s_of, 1)
                    dve.wait_ge(s_oh, i * 4 + (c + 1))
                    V.tensor_tensor(tile(o_lo, t), ot, tile(o_hi, t).bitcast(F32), ALU.subtract).then_inc(s_osp, 1)
            dve.wait_ge(s_gr["gg"], 16)
            with dve.Fori(0, 2) as i:
                for c in range(4):
                    n = Lin(at["ygla"] + c, 4, i)
                    t = i * 4 + c
                    step(n)
                    s = sg[:, c % 2, :]
                    V.scalar_tensor_tensor(halves(s), halves(tile(work_t, t)), 1.0, psum(c % 2),
                                           ALU.add, ALU.mult).then_inc(s_evac[c % 2], 1)
                    dve.wait_ge(s_evac[c % 2], n.half().value(1, 1))
                    V.tensor_tensor(s, s, tile(work_t, t + KT), ALU.add).then_inc(s_mf, 1)
                    dve.wait_ge(s_mh, i * 4 + (c + 1))
                    V.tensor_tensor(tile(h_lo, t), s, tile(h_hi, t).bitcast(F32), ALU.subtract).then_inc(s_mp, 1)
            dve.wait_ge(s_xr, 16)
            for i, k in bodies(dve, 2, 1):
                for c in range(4):
                    n = Lin(at["out"] + 4 * k + c, 4, i)
                    step(n)
                    residual(n, Lin(4 * k + c, 4, i).value(), GT2)
                    if i is not None or c:
                        add_square(3, Lin(4 * k + c - 1, 4, i))
            add_square(3, Lin(KT - 1))
            scale_of(SC3, "norm_ffn2")
            modulate(3, SC3, SH3)
            ffn(2, GT3)
            scale_of(SCF, "norm_final")
            modulate(4, SCF, SHF, final=True)


_INS = ["x_prompt", "x_sample", "c_prompt", "c_sample", "state_conv", "state_gla", "w_ada", "b_ada", "norm_ffn1",
        "ffn1_gate", "ffn1_up", "ffn1_down", "norm_mix", "w_in", "conv_w", "conv_b", "conv_ln_g", "conv_ln_b",
        "w_conv_out", "w_alpha", "b_alpha", "gla_norm", "w_gla_out", "w_out", "norm_ffn2", "ffn2_gate", "ffn2_up",
        "ffn2_down", "norm_final", "w_ada_final", "b_ada_final"]
_OUTS = {"y_prompt": (1, NP, D), "y_sample": (NS, 1, D), "conv_p": (1, 1, TAPS - 1, D),
         "gla_p": (1, 1, HEADS, DK, DV), "conv_s": (1, NS, TAPS - 1, D), "gla_s": (1, NS, HEADS, DK, DV)}


def kernel(**inputs):
    import concourse.bacc as bacc
    from concourse.bass_utils import run_bass_kernel_spmd as run

    nc = bacc.Bacc("TRN2", target_bir_lowering=False, num_devices=1)
    arrays = {f"in_{k}": np.ascontiguousarray(inputs[k]) for k in _INS}
    a = {k: nc.dram_tensor(f"in_{k}", arrays[f"in_{k}"].shape, F32, kind="ExternalInput").ap() for k in _INS}
    o = {k: nc.dram_tensor(f"out_{k}", s, F32, kind="ExternalOutput").ap() for k, s in _OUTS.items()}
    decoder_step(nc, a, o)
    r = run(nc, [arrays], core_ids=[0])
    return tuple(r.results[0][f"out_{k}"] for k in _OUTS)
```

```python
from contextlib import ExitStack

import numpy as np

import concourse.bass as bass
from concourse import mybir

F32 = mybir.dt.float32
F32R = mybir.dt.float32r
BF16 = mybir.dt.bfloat16
U16 = mybir.dt.uint16
ALU = mybir.AluOpType
ACT = mybir.ActivationFunctionType
AX_X = mybir.AxisListType.X

P = 128
D = 1024
KT = D // P
NP = 512
NS = 8
N = NP + NS
HALF = N // 2
FF = 2816
TAPS = 31
HEADS = 4
DK = 128
DV = 256
RANK = 16
CH = 128
NC = NP // CH
LEVELS = [64, 32, 16, 8, 4, 2, 1]
EPS = 1e-6
UP = TAPS - 1 + N
GROUPS = [8, 8, 6]
W_IN = {"ca": 0, "cb": 1024, "q": 2048, "k": 2560, "v": 3072, "r": 4096, "a": 5120,
        "gc": 5136, "gg": 6160}

VECS = ["norm_ffn1", "norm_mix", "norm_ffn2", "norm_final", "conv_b", "conv_ln_g", "conv_ln_b",
        "gla_norm", "b_alpha"]
VROW = {name: 8 * j for j, name in enumerate(VECS)}
NVEC = 8 * 8 + 4
TAPS_AT = [1, 2, 1, 1, 2, 0, 1, 2, 1, 2, 2, 0]
TAPS2_AT = [0, 0, 1, 1, 1, 2, 0, 0, 1, 1, 1, 0]
HIDDEN0 = 2
CONSTS = 30
CONSTS_START = 3
CONSTS_SMALL = 7
NADA = 88
(SH1, SC1, GT1, SH2, SC2, GT2, SH3, SC3, GT3, SHF, SCF) = range(11)


class Lin:

    def __init__(self, base, per=0, i=None):
        self.base, self.per, self.i = base, per, i

    def __add__(self, k):
        return Lin(self.base + k, self.per, self.i)

    def half(self):
        return Lin(self.base // 2, self.per // 2, self.i)

    def value(self, mul=1, add=0):
        v = self.base * mul + add
        return v if self.i is None else self.i * (self.per * mul) + v


class Chain:

    def __init__(self, eng, sem):
        self.eng, self.sem, self.n = eng, sem, Lin(0)

    def loop(self, i, per):
        self.n = Lin(self.n.base, per, i)
        self.start = self.n.base

    def end(self, turns):
        assert self.n.base - self.start == self.n.per, (self.n.base - self.start, self.n.per)
        self.n = Lin(self.start + self.n.per * turns)

    def mark(self, ins):
        ins.then_inc(self.sem, 1)
        self.n = self.n + 1

    def wait(self, back=0):
        self.eng.wait_ge(self.sem, self.n.value(add=-back))

    def link(self, ins):
        self.mark(ins)
        self.wait()


def bodies(eng, count, peel):
    if peel:
        yield None, 0
    with eng.Fori(0, count - peel) as i:
        yield i, peel


ADA0 = 10
ADA_SLABS = NADA // 2
ADA_UP = [ADA0, ADA0 + GROUPS[0] + 4, ADA0 + GROUPS[0] + GROUPS[1] + 8]
ADA_DOWN = [ADA_UP[g] + GROUPS[g] for g in range(3)]


def plan():
    at, n = {}, 0
    for name, units in ([(f"{w}1_{g}", u) for g in range(3) for w, u in (("up", GROUPS[g] * 2), ("down", 8))]
                        + [("conv", 16), ("alr", 4), ("qk", 8), ("v", 8), ("gates", 24),
                           ("yconv", 8), ("ygla", 8), ("out", 8)]
                        + [(f"{w}2_{g}", u) for g in range(3) for w, u in (("up", GROUPS[g] * 2), ("down", 8))]):
        at[name] = n
        n += units
    return at, n


def decoder_step(nc, a, o):
    at, UNITS = plan()
    A = {k: v for k, v in a.items()}

    with ExitStack() as ctx:
        def sb(name, shape, dt=F32):
            return ctx.enter_context(nc.sbuf_tensor(name, shape, dt))

        def overlay(*views):
            out = []
            for name, shape, dt in views[:-1]:
                with nc.sbuf_tensor(name, shape, dt) as t:
                    out.append(t)
            name, shape, dt = views[-1]
            out.append(sb(name, shape, dt))
            return out

        def sem(name):
            return ctx.enter_context(nc.semaphore(name))

        raw = sb("raw", [P, 2, KT, 256])
        w_hi = [sb(f"w_hi{p}", [P, KT, P], F32R) for p in range(2)]
        w_lo = [sb(f"w_lo{p}", [P, KT, P], F32R) for p in range(2)]
        h_hi = sb("h_hi", [P, KT, N], F32R)
        h_lo = sb("h_lo", [P, KT, N], F32R)
        x = sb("x", [P, KT, N])
        BF = 2 * KT * N
        lay = {}
        off = 0
        for name, cols in (("E", 2 * NP), ("M", 2 * N), ("EB", N), ("QS", NP), ("SC", NP), ("KTK", NP),
                           ("VH", NC * DV), ("SB", NC * DV), ("ST", NS * DV)):
            lay[name] = (off, off + cols)
            off += cols
        assert off <= BF
        f_hl = []
        with ExitStack() as c2:
            for nm in ("f_hi", "f_lo"):
                f_hl.append(c2.enter_context(nc.sbuf_tensor(nm, [P, KT, N], F32R)))
        f_hi, f_lo = f_hl
        work = sb("work", [P, BF])

        def wk(name):
            return work[:, lay[name][0]:lay[name][1]]

        E_ = wk("E").rearrange("p (b n) -> p b n", b=2)
        M_ = wk("M").rearrange("p (b n) -> p b n", b=2)
        EB = wk("EB")
        QS = wk("QS")
        SC = wk("SC")
        KTK = wk("KTK").rearrange("p (c n) -> p c n", c=NC)
        VH = wk("VH").rearrange("p (c n) -> p c n", c=NC)
        SB = wk("SB").rearrange("p (c n) -> p c n", c=NC)
        ST = wk("ST").rearrange("p (b n) -> p b n", b=NS)
        raw_w = work[:, 0:4 * KT * 256].rearrange("p (s k n) -> p s k n", s=4, k=KT)
        work_t = work[:].rearrange("p (t n) -> p t n", t=2 * KT)
        t_gg, t_gc = work_t[:, 0:KT, :], work_t[:, KT:, :]

        wa0, qk = overlay(("wa0", [P, 2, KT, 256], F32R), ("qk", [P, KT, N], F32))
        xtok, convs, vtok, ytok, o_lo = overlay(
            ("xtok", [P, 4, D], F32), ("convs", [P, 2 * D + KT * NS * TAPS], F32),
            ("vtok", [P, NC, D], F32), ("ytok", [P, 4, D], F32), ("o_lo", [P, KT, N], F32R))
        rows, wa1, o_hi, u = overlay(("rows", [P, 2 * D + 4 * P], F32), ("wa1", [P, 2, KT, 256], F32R),
                                ("o_hi", [P, KT, N], F32R),
                                ("u", [P, KT, UP], F32))
        raw_a, d = overlay(("raw_a", [P, 2, KT, 256], F32), ("d", [P, KT, N], F32))
        lb = sb("lb", [P, HEADS, N])
        wa = [wa0, wa1]
        rows_a = lb[0:20, 0:2, 0:256]
        sg = sb("sg", [P, 4, N])
        mod = sb("mod", [P, NADA, 10])
        vt = sb("vt", [P, NVEC + NADA])
        cw = sb("cw", [P, TAPS * KT])
        masks = sb("masks", [P, len(LEVELS) + 1, P], BF16)
        ident = sb("ident", [P, P])
        ones = sb("ones", [P, P])
        sel = sb("sel", [20, 10])
        eps = sb("eps", [P, 1])
        c_f = sb("c_f", [P, KT, 10])
        c_hl = sb("c_hl", [P, KT, 20], F32R)
        t8 = sb("t8", [P, 2, NS])
        hs = sb("hs", [P, KT, NS])
        ks8 = sb("ks8", [NS, DK])
        walpha, alr = work[0:RANK, 0:HEADS * DK], work[0:RANK, HEADS * DK:HEADS * DK + N]
        x_rows = x[0:NS, 0:4, :].rearrange("p a n -> p (a n)")
        vs, km = x_rows[:, 0:D], x_rows[:, D:2 * D].rearrange("p (b n) -> p b n", b=NS)
        x_rows_d = nc.dram_tensor("x_rows_d", [NS, 4 * N], F32, kind="Internal").ap()
        ysrow = d[0:NS, 0:2, :].rearrange("p a n -> p (a n)")[:, 0:D]
        crow = rows[0:9, 0:D]
        xsrow = rows[0:NS, D:2 * D]
        vrow = rows[0:NVEC, 2 * D:2 * D + P]
        brow = rows[0:NADA, 2 * D + P:2 * D + 2 * P]
        cwrow = rows[0:TAPS * 4, 2 * D + 2 * P:2 * D + 4 * P].rearrange("p (g n) -> p g n", g=2)
        srow = convs[0:120, 0:2 * D].rearrange("p (g n) -> p g n", g=2)
        sT = convs[:, 2 * D:].rearrange("p (t b j) -> p t b j", t=KT, b=NS)

        def ada_slot(m):
            if m.i is None and m.base < ADA0:
                slot, loads = m.base % 6, Lin(m.base // 6 + 1)
            else:
                slot = m.base % 2
                loads = (m + (-ADA0 - slot)).half() + (ADA0 + 5) // 6 + 1
            return raw_a[:, slot] if slot < 2 else raw_w[:, slot - 2], s_araw[slot], loads.value(16)

        pu = [ctx.enter_context(nc.psum_tensor(f"pu{p}", [P, 2, 512], F32)) for p in range(2)]
        pg = ctx.enter_context(nc.psum_tensor("pg", [P, 4, 512], F32))

        gates_d = nc.dram_tensor("gates_d", [3, KT, P, N], F32, kind="Internal").ap()

        def sems(**names):
            return {k: sem(v) for k, v in names.items()}

        s_raw = [sem("raw0_loaded"), sem("raw1_loaded")]
        s_free = sem("raw_slabs_found_free")
        s_hi, s_lo, s_done = sem("w_hi_ready"), sem("w_lo_ready"), sem("unit_done")
        s_evac = [sem("even_unit_out_of_psum"), sem("odd_unit_out_of_psum")]
        s_const = sem("consts_ready")
        s_ld = {k: sem("loaded_" + k) for k in ("x", "c", "xs", "vec", "b", "cw", "st", "wa")}
        s_tp, s_te, s_td = sem("start_transposed"), sem("start_read_by_act"), sem("start_read_by_dve")
        s_cf, s_c = sem("c_ready"), sem("c_split")
        s_araw = [sem(f"ada_raw{j}_loaded") for j in range(6)]
        s_afree = sem("ada_slabs_found_free")
        s_wah, s_wal, s_ad = sem("ada_hi_ready"), sem("ada_lo_ready"), sem("ada_rows_in_psum")
        s_ar, s_at, s_mod = sem("ada_rows_ready"), sem("ada_rows_transposed"), sem("modulation_ready")
        s_sq, s_sqf, s_ss = sem("square_ready"), sem("square_added"), sem("sums_in_psum")
        s_root, s_rstd, s_xn = sem("root_ready"), sem("rstd_ready"), sem("x_times_rstd")
        s_hf, s_hh, s_h = sem("h_full"), sem("h_hi_ready"), sem("h_split")
        s_ln = sem("conv_tiles_added")
        s_cen = sem("conv_tile_centered")
        s_ahi, s_a, s_x = sem("hidden_hi_ready"), sem("hidden_split"), sem("x_updated")
        s_ct, s_cts, s_cst = sem("u_tails_transposed"), sem("u_tails_staged"), sem("u_tails_stored")
        s_cvt, s_cve, s_cvs = sem("state_conv_transposed"), sem("state_conv_read"), sem("sample_conv_done")
        s_cv = sem("conv_step")
        s_cpy = sem("state_conv_copied")
        s_xsp, s_xr = sem("x_rows_spilled"), sem("x_rows_restored")
        s_lg, s_z, s_az = sem("logits_ready"), sem("z_ready"), sem("abs_z_ready")
        s_l, s_b = sem("log1p_ready"), sem("b_ready")
        s_vt, s_v = sem("v_transposed"), sem("vtok_ready")
        s_gt = sem("r_tanh_ready")
        s_gsp = [sem(f"gate_spilled{j}") for j in range(4)]
        s_gr = {k: sem("gate_reloaded_" + k) for k in ("r", "gc", "gg")}
        s_gd, s_ge, s_gk = sem("gla_diff_ready"), sem("gla_exp_ready"), sem("gla_v_head_ready")
        s_gm, s_gg, s_gp = sem("gla_mix_ready"), sem("gla_gram_ready"), sem("gla_scores_merged")
        s_merge = sem("gla_scores_free_to_merge")
        s_kt, s_kr, s_km = sem("gla_k_transposed"), sem("gla_k_read"), sem("sample_k_masked")
        s_ds, s_S = sem("gla_ds_ready"), sem("gla_state_ready")
        s_ko, s_sn = sem("sample_outer_ready"), sem("sample_state_ready")
        s_o, s_oe = sem("gla_o_ready"), sem("gla_o_read")
        s_st, s_sto, s_So = sem("state_loaded"), sem("sample_state_stored"), sem("prompt_state_stored")
        s_osq, s_os, s_ol = sem("o_squares_ready"), sem("o_sums_in_psum"), sem("o_logs_ready")
        s_om, s_or = sem("o_root_ready"), sem("o_rstd_ready")
        s_ox, s_of, s_oh, s_osp = sem("o_normed"), sem("o_gated"), sem("o_hi_ready"), sem("o_split")
        s_mf, s_mh, s_mp = sem("merged_ready"), sem("merged_hi_ready"), sem("merged_split")
        s_yn, s_yt, s_ye, s_fin = sem("y_ready"), sem("y_transposed"), sem("y_staged"), sem("y_stored")
        s_ys, s_yse = sem("sample_y_ready"), sem("sample_y_staged")
        s_dv, s_ac = sem("dve_step"), sem("act_step")

        block = ctx.enter_context(nc.Block())
        w_ada, w_in = A["w_ada"][0], A["w_in"][0]
        MIX = {"k": 1, "qs": 2, 7: 10} | {l: l + 3 for l in range(7)}

        def flat(v):
            return v.rearrange("p o n -> p (o n)")

        def tile(t, n, a=0, b=N):
            return flat(t[:, bass.ds(n, 1), a:b])

        def halves(v):
            return v.rearrange("p (e n) -> p e n", e=2)

        @block.sync
        def _(sp):
            def cols(w, c, k=KT, r0=0):
                v = w[r0:r0 + k * P, :].rearrange("(k p) n -> p k n", p=P)
                return v[:, :, bass.ds(c if isinstance(c, int) else sp.snap(c), 256)]

            def load(n, slot, src, k=KT):
                if n.i is not None or n.base >= 4:
                    sp.wait_ge(s_lo, n.value(add=-2))
                    sp.sem_inc(s_free, 1)
                sp.dma_start(raw[:, slot, 0:k, :], src).then_inc(s_raw[slot], 16)

            def pair(n, w, c, c2=None, k=KT, r0=0):
                load(n, 0, cols(w, c, k, r0), k)
                w2, c2 = c2 if c2 is not None else (w, c + 256)
                load(n + 2, 1, cols(w2, c2, k, r0), k)

            def ffn(which):
                wg, wu, wd = (A[f"ffn{which}_{w}"][0] for w in ("gate", "up", "down"))
                for g in range(3):
                    r0 = sum(GROUPS[:g]) * P
                    n0 = at[f"up{which}_{g}"]
                    for i, k in bodies(sp, GROUPS[g] // 2, n0 == 0):
                        c = r0 if i is None else i * 256 + (r0 + 256 * k)
                        pair(Lin(n0 + 4 * k, 4, i), wg, c, (wu, c))
                    with sp.Fori(0, 2) as i:
                        pair(Lin(at[f"down{which}_{g}"], 4, i), wd, i * 512, k=GROUPS[g], r0=r0)

            sp.wait_ge(s_ld["x"], 64)
            ffn(1)
            with sp.Fori(0, 4) as i:
                pair(Lin(at["conv"], 4, i), w_in, i * 256 + W_IN["cb"], (w_in, i * 256 + W_IN["ca"]))
            pair(Lin(at["alr"]), w_in, W_IN["a"], (w_in, W_IN["a"]))
            for name, w, c in (("qk", w_in, W_IN["q"]), ("v", w_in, W_IN["v"])):
                with sp.Fori(0, 2) as i:
                    pair(Lin(at[name], 4, i), w, i * 512 + c)
            with sp.Fori(0, 2) as i:
                for j, g in enumerate(("r", "gc", "gg")):
                    pair(Lin(at["gates"] + 4 * j, 12, i), w_in, i * 512 + W_IN[g])
            for name, w in (("yconv", "w_conv_out"), ("ygla", "w_gla_out"), ("out", "w_out")):
                with sp.Fori(0, 2) as i:
                    pair(Lin(at[name], 4, i), A[w][0], i * 512)
            ffn(2)

            yp = o["y_prompt"][0].rearrange("(c p) d -> p c d", p=P)
            for a, b in ((0, 4), (4, 6), (6, 8)):
                sp.wait_ge(s_ye, b)
                sp.dma_start(yp[:, :, a * P:b * P], ytok[:, :, a * P:b * P]).then_inc(s_fin, 16)
            sp.wait_ge(s_yse, 1)
            sp.dma_start(o["y_sample"].rearrange("b t d -> (b t) d"), ysrow).then_inc(s_fin, 16)
            sp.wait_ge(s_fin, 64)

        @block.gpsimd
        def _(pool):
            def ada_load(m, w, c):
                if m.i is not None or m.base >= ADA0:
                    pool.wait_ge(s_wal, m.value(add=-1))
                    pool.sem_inc(s_afree, 1)
                elif m.base >= 6:
                    pool.wait_ge(s_wal, m.base - 5)
                dst, s_loaded, _ = ada_slot(m)
                v = w.rearrange("(k p) n -> p k n", p=P)
                pool.dma_start(dst, v[:, :, bass.ds(c, 256)]).then_inc(s_loaded, 16)

            nc.gpsimd.memset(ident[:], 0.0).then_inc(s_const, 1)
            nc.gpsimd.memset(ones[:], 1.0).then_inc(s_const, 1)
            pool.wait_ge(s_const, 1)
            nc.gpsimd.affine_select(out=ident[:], in_=ident[:], compare_op=ALU.not_equal, fill=1.0,
                                    base=0, pattern=[[-1, P]], channel_multiplier=1).then_inc(s_const, 1)
            ada_load(Lin(0), w_ada, 0)
            nc.gpsimd.memset(sel[:], 0.0).then_inc(s_const, 1)
            for j in range(2):
                pool.wait_ge(s_const, CONSTS_START + 1 + j)
                nc.gpsimd.affine_select(out=sel[:], in_=sel[:], compare_op=ALU.not_equal, fill=1.0,
                                        base=-10 * j, pattern=[[-1, 10]], channel_multiplier=1).then_inc(s_const, 1)
            nc.gpsimd.memset(eps[:], EPS).then_inc(s_const, 1)
            pool.wait_ge(s_ld["x"], 64)
            for m in range(1, 6):
                ada_load(Lin(m), w_ada, m * 256)
            nc.gpsimd.memset(masks[:], 0.0).then_inc(s_const, 1)
            n = CONSTS_SMALL + 1
            pool.wait_ge(s_const, n)
            for l, h in enumerate(LEVELS):
                v = masks[:, l, :].rearrange("p (b e t) -> p b e t", e=2, t=h)
                nc.gpsimd.memset(v[:, :, 1, :], 1.0).then_inc(s_const, 1)
                n += 1
                for base, step in ((0, 1), (h - 1, -1)):
                    pool.wait_ge(s_const, n)
                    nc.gpsimd.affine_select(out=v, in_=v, compare_op=ALU.is_ge, fill=0.0, base=base,
                                            pattern=[[-step * 2 * h, P // (2 * h)], [0, 2], [0, h]],
                                            channel_multiplier=step).then_inc(s_const, 1)
                    n += 1
            nc.gpsimd.affine_select(out=masks[:, 7, :], in_=masks[:, 7, :], compare_op=ALU.not_equal,
                                    fill=1.0, base=0, pattern=[[-1, P]], channel_multiplier=1
                                    ).then_inc(s_const, 1)
            assert n + 1 == CONSTS
            for m in range(6, ADA0):
                ada_load(Lin(m), w_ada, m * 256)
            with pool.Fori(0, (36 - ADA0) // 2) as i:
                for j in range(2):
                    ada_load(Lin(ADA0 + j, 2, i), w_ada, i * 512 + 256 * (ADA0 + j))
            with pool.Fori(0, 4) as i:
                for j in range(2):
                    ada_load(Lin(36 + j, 2, i), A["w_ada_final"], i * 512 + 256 * j)

            pool.dma_start(o["conv_s"][0, :, 0:TAPS - 2, :], A["state_conv"][0, :, 1:TAPS - 1, :]
                           ).then_inc(s_cpy, 16)
            pool.wait_ge(s_te, 1 + KT)
            rows_st = A["state_conv"][0].rearrange("(g b) j f -> g (b j) f", g=2)
            for g in range(2):
                pool.dma_start(convs[0:120, g * D:(g + 1) * D], rows_st[g]).then_inc(s_ld["st"], 16)
            st_in = A["state_gla"][0].rearrange("b h k v -> h k b v")
            st_out = o["gla_s"][0].rearrange("b h k v -> h k b v")
            pool.wait_ge(s_done, at["conv"])
            pool.dma_start(walpha, A["w_alpha"][0]).then_inc(s_ld["wa"], 16)
            pool.dma_start(ST, st_in[0]).then_inc(s_st, 16)
            pool.wait_ge(s_x, 3 * KT)
            pool.dma_start(x_rows_d, x_rows).then_inc(s_xsp, 16)
            pool.wait_ge(s_cts, 1)
            pool.dma_start(o["conv_p"][0, 0], flat(sg[:])[0:TAPS - 1, 0:D]).then_inc(s_cst, 16)
            pool.dma_start(o["conv_s"][0, :, TAPS - 2, :], flat(sg[:])[TAPS - 1:TAPS - 1 + NS, 0:D]
                           ).then_inc(s_cst, 16)
            for h in range(HEADS):
                pool.wait_ge(s_S, 4 * h + 4)
                pool.dma_start(o["gla_p"][0, 0, h], SB[:, 3, :]).then_inc(s_So, 16)
                pool.wait_ge(s_oe, 2 * h + 1)
                pool.dma_start(st_out[h], ST).then_inc(s_sto, 16)
                pool.wait_ge(s_So, 16 * (h + 1))
                pool.wait_ge(s_sto, 16 * (h + 1))
                if h + 1 < HEADS:
                    pool.dma_start(ST, st_in[h + 1]).then_inc(s_st, 16)
            pool.wait_ge(s_oe, 2 * HEADS)
            pool.wait_ge(s_xsp, 16)
            pool.dma_start(x_rows, x_rows_d).then_inc(s_xr, 16)
            for j in range(4):
                pool.wait_ge(s_gsp[j], 6 * 16)
            back = [gates_d[j].rearrange("t p n -> p t n") for j in range(3)]
            pool.dma_start(t_gc, back[1]).then_inc(s_gr["gc"], 16)
            pool.wait_ge(s_h, 3 * KT)
            pool.dma_start(d[:], back[0]).then_inc(s_gr["r"], 16)
            pool.wait_ge(s_os, HEADS)
            pool.dma_start(t_gg, back[2]).then_inc(s_gr["gg"], 16)
            pool.wait_ge(s_cst, 32)
            pool.wait_ge(s_cpy, 16)

        @block.tensor
        def _(pe):
            mm = nc.tensor.matmul

            def weights_and_psum(n, p):
                pe.wait_ge(s_lo, n.value(add=1))
                if n.i is not None or n.base >= 2:
                    pe.wait_ge(s_evac[p], n.half().value())

            def unit(n, p, hi, lo, k_tiles=KT, ready=None, done=1):
                weights_and_psum(n, p)
                for k in range(k_tiles):
                    if ready is not None:
                        s, v, first = ready
                        if k == 0 and first > 1:
                            pe.wait_ge(s, v + first)
                        elif k >= first or k == 0:
                            pe.wait_ge(s, v + k + 1)
                    for j, (w, m) in enumerate(((w_hi, hi), (w_hi, lo), (w_lo, hi))):
                        for e in range(2):
                            last = mm(pu[p][:, e, 0:HALF], w[p][:, k, :], m[:, k, e * HALF:(e + 1) * HALF],
                                      start=(k == 0 and j == 0), stop=(k == k_tiles - 1 and j == 2))
                last.then_inc(s_done, done)

            def unit_pair(n, hi, lo, s, v):
                for p in range(2):
                    weights_and_psum(n + p, p)
                for k in range(KT):
                    pe.wait_ge(s, v + k + 1)
                    for p in range(2):
                        for j, (w, m) in enumerate(((w_hi, hi), (w_hi, lo), (w_lo, hi))):
                            for e in range(2):
                                last = mm(pu[p][:, e, 0:HALF], w[p][:, k, :], m[:, k, e * HALF:(e + 1) * HALF],
                                          start=(k == 0 and j == 0), stop=(k == KT - 1 and j == 2))
                        if k == KT - 1:
                            last.then_inc(s_done, 1)

            def ada(m):
                slot = m.base % 2
                if m.i is not None or m.base >= 2:
                    pe.wait_ge(s_ar, m.value(add=-1))
                pe.wait_ge(s_wal, m.value(1, 1))
                for k in range(KT):
                    for j in range(2):
                        last = mm(pg[0:20, 2 + slot, 0:256], c_hl[:, k, :], wa[slot][:, j, k, :],
                                  start=(k == 0 and j == 0), stop=(k == KT - 1 and j == 1))
                last.then_inc(s_ad, 1)

            def ada_transpose(m):
                slot = m.base % 2
                if m.i is not None or m.base >= 2:
                    pe.wait_ge(s_mod, m.value(add=-1))
                pe.wait_ge(s_ar, m.value(1, 1))
                for e in range(2):
                    last = mm(pg[:, slot, 10 * e:10 * e + 10], rows_a[:, slot, e * P:(e + 1) * P], sel[:],
                              start=True, stop=True)
                last.then_inc(s_at, 1)

            def sums(src, b=0):
                for e in range(2):
                    last = mm(pg[:, b + e, 0:HALF], ones[:], src[:, e * HALF:(e + 1) * HALF],
                              start=True, stop=True)
                return last

            def norm_sums(q):
                pe.wait_ge(s_sqf, KT * (q + 1))
                sums(sg[:, 2, :]).then_inc(s_ss, 1)

            pe.wait_ge(s_const, CONSTS_START)
            pe.wait_ge(s_ld["c"], 32)
            for t in range(KT):
                last = nc.tensor.transpose(pg[:, 0, 10 * t:10 * t + 9], crow[:, t * P:(t + 1) * P], ident[0:9, 0:9])
            last.then_inc(s_tp, 1)
            pe.wait_ge(s_ld["vec"], 16 * len(VECS))
            pe.wait_ge(s_ld["b"], 32)
            pe.wait_ge(s_ld["cw"], 32)
            nc.tensor.transpose(pg[:, 1, 0:NVEC], vrow, ident[0:NVEC, 0:NVEC])
            nc.tensor.transpose(pg[:, 1, NVEC:NVEC + NADA], brow, ident[0:NADA, 0:NADA])
            for g in range(2):
                last = nc.tensor.transpose(pg[:, 1, 160 + g * 124:160 + g * 124 + 124], cwrow[:, g, :],
                                           ident[0:124, 0:124])
            last.then_inc(s_tp, 1)
            pe.wait_ge(s_ld["x"], 64)
            pe.wait_ge(s_ld["xs"], 16)
            for t in range(KT):
                b = t % 2
                if t >= 2:
                    pe.wait_ge(s_te, t)
                    pe.wait_ge(s_td, t)
                for c in range(4):
                    nc.tensor.transpose(pg[:, 2 + b, c * P:(c + 1) * P], xtok[:, c, t * P:(t + 1) * P], ident[:])
                if t == 0:
                    pe.wait_ge(s_te, 1)
                if t == 1:
                    pe.wait_ge(s_td, 1)
                nc.tensor.transpose(pg[:, b, 0:NS], xsrow[:, t * P:(t + 1) * P], ident[0:NS, 0:NS]
                                    ).then_inc(s_tp, 1)
            pe.wait_ge(s_c, 2)
            pe.wait_ge(s_te, 1 + KT)
            pe.wait_ge(s_td, 1 + KT)
            pe.wait_ge(s_const, CONSTS_SMALL)
            ada(Lin(0))
            ada(Lin(1))
            norm_sums(0)
            ada(Lin(2))
            ada(Lin(3))
            pe.wait_ge(s_rstd, 1)
            ada_transpose(Lin(0))
            ada_transpose(Lin(1))
            for m in range(4, ADA0):
                ada_transpose(Lin(m - 2))
                ada(Lin(m))
            ada_transpose(Lin(ADA0 - 2))
            ada_transpose(Lin(ADA0 - 1))
            pe.wait_ge(s_const, CONSTS)

            def ffn(which):
                def ada_part(c, m, i):
                    if which == 1:
                        (ada_transpose if c % 2 else ada)(Lin(m + c // 2, 2, i))

                for g in range(3):
                    n0 = at[f"up{which}_{g}"]
                    for i, k in bodies(pe, GROUPS[g] // 2, g == 0):
                        if g == 0 and i is None:
                            unit_pair(Lin(n0), h_hi, h_lo, s_h, (which - 1) * 3 * KT)
                        for c in range(4):
                            if g or i is not None or c >= 2:
                                unit(Lin(n0 + 4 * k + c, 4, i), c % 2, h_hi, h_lo)
                            ada_part(c, ADA_UP[g] + 2 * k, i)
                    a0 = HIDDEN0 + (which - 1) * (FF // P) + sum(GROUPS[:g])
                    with pe.Fori(0, 2) as i:
                        for c in range(4):
                            unit(Lin(at[f"down{which}_{g}"] + c, 4, i), c % 2, f_hi, f_lo, GROUPS[g],
                                 ready=(s_a, a0, GROUPS[g] - 1) if c == 0 else None)
                            ada_part(c, ADA_DOWN[g], i)

            ffn(1)
            pe.wait_ge(s_mod, ADA_SLABS)
            norm_sums(1)

            def state_transposes(t0):
                pe.wait_ge(s_ld["st"], 32)
                pe.wait_ge(s_rstd, 2)
                for t in range(t0, t0 + 4):
                    if t >= 4:
                        pe.wait_ge(s_cve, t - 3)
                    transpose_state(t)

            def transpose_state(t):
                for g in range(2):
                    last = nc.tensor.transpose(pg[:, t % 4, g * 120:(g + 1) * 120],
                                               convs[0:120, g * D + t * P:g * D + (t + 1) * P], ident[0:120, 0:120])
                last.then_inc(s_cvt, 1)

            for i, k in bodies(pe, 4, 1):
                if i is None:
                    unit_pair(Lin(at["conv"]), h_hi, h_lo, s_h, KT)
                for c in range(4):
                    if i is not None or c >= 2:
                        unit(Lin(at["conv"] + 4 * k + c, 4, i), c % 2, h_hi, h_lo)
                    if i is None and c >= 2:
                        state_transposes(4 * (c - 2))
            n = at["alr"]
            pe.wait_ge(s_evac[1], n // 2)
            unit(Lin(n), 0, h_hi, h_lo, done=4)
            def u_tails():
                pe.wait_ge(s_cve, KT)
                pe.wait_ge(s_evac[1], at["alr"] // 2)
                for t in range(KT):
                    last = nc.tensor.transpose(pg[0:TAPS - 1 + NS, t // 4, (t % 4) * P:(t % 4 + 1) * P],
                                               u[:, t, NP:UP], ident[:])
                last.then_inc(s_ct, 1)

            def logits(h):
                b = 2 * (h % 2)
                if h == 0:
                    pe.wait_ge(s_evac[0], at["alr"] // 2 + 2)
                    pe.wait_ge(s_ld["wa"], 16)
                    pe.wait_ge(s_cts, 1)
                elif h >= 2:
                    pe.wait_ge(s_z, h - 1)
                for e in range(2):
                    last = mm(pg[:, b + e, 0:HALF], walpha[:, h * DK:(h + 1) * DK],
                              alr[:, e * HALF:(e + 1) * HALF], start=True, stop=True)
                last.then_inc(s_lg, 1)

            for i, k in bodies(pe, 2, 1):
                for c in range(4):
                    unit(Lin(at["qk"] + 4 * k + c, 4, i), c % 2, h_hi, h_lo)
                    if i is None and c == 0:
                        u_tails()
                    if i is None and c in (1, 2):
                        logits(2 * c - 2)
                        logits(2 * c - 1)
            pe.wait_ge(s_z, HEADS)
            def v_transposes(i, k, e):
                for p in range(2):
                    pe.wait_ge(s_evac[p], Lin(at["v"] + 4 * k + 2 * e, 4, i).half().value(add=1))
                if i is not None or e:
                    pe.wait_ge(s_v, Lin(2 * k + e, 2, i).value())
                for t in range(2):
                    for c in range(NC):
                        q = c * DV + t * P
                        nc.tensor.transpose(pg[:, q // 512, q % 512:q % 512 + P],
                                            sg[:, 2 * e + t, c * CH:(c + 1) * CH], ident[:])
                    last = nc.tensor.transpose(pg[0:NS, 2, t * P:(t + 1) * P], sg[:, 2 * e + t, NP:N], ident[:])
                last.then_inc(s_vt, 1)

            for i, k in bodies(pe, 2, 1):
                for c in range(4):
                    unit(Lin(at["v"] + 4 * k + c, 4, i), c % 2, h_hi, h_lo)
                    if c >= 2:
                        v_transposes(i, k, c - 2)

            def gram(h, l, rhs=None):
                pe.wait_ge(s_gm, h.value(10, MIX[l]))
                if l >= 2:
                    pe.wait_ge(s_gp, h.value(8, l - 1))
                for c in range(NC):
                    m = M_[:, l % 2, c * CH:(c + 1) * CH]
                    last = mm(pg[:, l % 2, c * CH:(c + 1) * CH], m,
                              m if rhs is None else rhs[:, c * CH:(c + 1) * CH], start=True, stop=True)
                last.then_inc(s_gg, 1)

            def k_transposes(h):
                pe.wait_ge(s_gm, h.value(10, MIX["k"]))
                for c in range(NC):
                    nc.tensor.transpose(pg[:, 2, c * CH:(c + 1) * CH], M_[:, 0, c * CH:(c + 1) * CH], ident[:])
                nc.tensor.transpose(pg[0:NS, 3, 0:DK], M_[:, 0, NP:N], ident[:]).then_inc(s_kt, 1)

            def chunk_states(h):
                pe.wait_ge(s_kr, h.value(2, 2))
                pe.wait_ge(s_gk, h.value(1, 1))
                for c in range(NC):
                    last = mm(pg[:, 2 + c // 2, (c % 2) * DV:(c % 2 + 1) * DV], KTK[:, c, :], VH[:, c, :],
                              start=True, stop=True)
                last.then_inc(s_ds, 1)

            def outer_ready(h, r):
                pe.wait_ge(s_km, h.value(1, 1))
                if r == 0:
                    pe.wait_ge(s_S, h.value(4, 4))
                else:
                    pe.wait_ge(s_sn, h.value(8, 4))

            def sample_outer(h, r):
                for b in range(4):
                    last = mm(pg[:, 2 + b // 2, (b % 2) * DV:(b % 2 + 1) * DV], km[:, 4 * r + b, :],
                              vs[:, bass.ds(h.value(DV), DV)], start=True, stop=True)
                last.then_inc(s_ko, 1)

            def sample_o(h):
                pe.wait_ge(s_sn, h.value(8, 8))
                q = tile(qk, h.value(2))
                for t in range(2):
                    for b in range(NS):
                        last = mm(pg[:, 2, t * NS + b:t * NS + b + 1], ST[:, b, t * P:(t + 1) * P],
                                  q[:, NP + b:NP + b + 1], start=True, stop=True)
                last.then_inc(s_o, 1)

            def prompt_o(h):
                pe.wait_ge(s_gp, h.value(8, 8))
                pe.wait_ge(s_oe, h.value(2, 1))
                for t in range(2):
                    for c in range(NC):
                        cs, ts = slice(c * CH, (c + 1) * CH), slice(t * P, (t + 1) * P)
                        last = mm(pg[:, 2 + t, cs], VH[:, c, ts], SC[:, cs], start=True, stop=(c == 0))
                        if c:
                            last = mm(pg[:, 2 + t, cs], SB[:, c - 1, ts], QS[:, cs], start=False, stop=True)
                last.then_inc(s_o, 1)

            with pe.Fori(0, 2) as i:
                for hh in range(2):
                    h = Lin(hh, 2, i)
                    for s in range(6):
                        unit(Lin(at["gates"] + 6 * hh + s, 12, i), s % 2, h_hi, h_lo)
                        if s == 1:
                            k_transposes(h)
                        if s == 2:
                            chunk_states(h)
                            gram(h, 0)
                            gram(h, 1)
                        if s == 3:
                            outer_ready(h, 0)
                            gram(h, 2)
                            sample_outer(h, 0)
                            gram(h, 3)
                        if s == 4:
                            outer_ready(h, 1)
                            gram(h, 4)
                            sample_outer(h, 1)
                            gram(h, 5)
                        if s == 5:
                            gram(h, 6)
                            gram(h, 7, tile(qk, h.value(2)))
                            sample_o(h)
                            prompt_o(h)

            pe.wait_ge(s_ln, 2)
            pe.wait_ge(s_oe, 2 * HEADS)
            sums(sg[:, 2, :]).then_inc(s_ss, 1)
            norm_sums(2)
            def o_sums(h):
                pe.wait_ge(s_osq, h + 1)
                pe.wait_ge(s_rstd, 3)
                if h >= 2:
                    pe.wait_ge(s_or, h - 1)
                for e in range(2):
                    for t in range(2):
                        last = mm(pg[:, 2 * (h % 2) + e, 0:HALF], ones[:],
                                  work_t[:, 2 * h + t, e * HALF:(e + 1) * HALF], start=(t == 0), stop=(t == 1))
                last.then_inc(s_os, 1)

            for i, k in bodies(pe, 2, 1):
                for c in range(4):
                    if i is None and c in (0, 2):
                        o_sums(c)
                        o_sums(c + 1)
                    unit(Lin(at["yconv"] + 4 * k + c, 4, i), c % 2, h_hi, h_lo,
                         ready=(s_h, 2 * KT, 1) if c == 0 else None)
            for name, hi, lo, s, v in (("ygla", o_hi, o_lo, s_osp, 0),
                                       ("out", h_hi, h_lo, s_mp, 0)):
                with pe.Fori(0, 2) as i:
                    for c in range(4):
                        unit(Lin(at[name] + c, 4, i), c % 2, hi, lo, ready=(s, v, 1) if c == 0 else None)
            norm_sums(3)
            ffn(2)
            norm_sums(4)
            pe.wait_ge(s_ys, 1)
            for t in range(KT):
                last = nc.tensor.transpose(pu[0][0:NS, t // 4, (t % 4) * P:(t % 4 + 1) * P], x[:, t, NP:N], ident[:])
            last.then_inc(s_yt, 1)
            for t in range(KT):
                pe.wait_ge(s_yn, t + 1)
                if t >= 4:
                    pe.wait_ge(s_ye, t - 3)
                for c in range(4):
                    last = nc.tensor.transpose(pg[:, t % 4, c * P:(c + 1) * P], x[:, t, c * P:(c + 1) * P], ident[:])
                last.then_inc(s_yt, 1)

        @block.scalar
        def _(act):
            af = nc.scalar.activation
            chain = Chain(act, s_ac)

            def split_hi(n, p, slot):
                act.wait_ge(s_raw[slot], n.half().half().value(16, 16))
                nc.scalar.copy(w_hi[p][:], raw[:, slot, :, p * P:(p + 1) * P]).then_inc(s_hi, 1)

            def step(n, more=True):
                act.wait_ge(s_done, n.value(1, 1))
                if more:
                    c = n.base % 4
                    split_hi(n + 2, c % 2, ((c + 2) // 2) % 2)

            def ada_split(m):
                if m.i is not None or m.base >= 2:
                    act.wait_ge(s_ad, m.value(add=-1))
                src, s_loaded, v = ada_slot(m)
                act.wait_ge(s_loaded, v)
                nc.scalar.copy(wa[m.base % 2][:, 0], src).then_inc(s_wah, 1)

            def ada_rows(m):
                slot = m.base % 2
                if m.i is not None or m.base >= 2:
                    act.wait_ge(s_at, m.value(add=-1))
                act.wait_ge(s_ad, m.value(1, 1))
                nc.scalar.copy(rows_a[:, slot], pg[0:20, 2 + slot, 0:256]).then_inc(s_ar, 1)

            def psum(p):
                return pu[p][:, :, 0:HALF]

            def square(q, t, src, s=None, v=0):
                if t.i is not None or t.base >= 2:
                    act.wait_ge(s_sqf, t.value(add=KT * q - 1))
                if s is not None:
                    act.wait_ge(s, t.value(add=v + 1))
                af(sg[:, t.base % 2, :], tile(src, t.value()), ACT.Square).then_inc(s_sq, 1)

            def rstd(ss):
                act.wait_ge(s_ss, ss)
                chain.link(af(halves(sg[:, 3, :]), pg[:, 0:2, 0:HALF], ACT.Ln, scale=1 / D, bias=eps[:]))
                af(sg[:, 3, :], sg[:, 3, :], ACT.Exp, scale=-0.5).then_inc(s_root, 1)

            def modulate(j, sc, sh):
                for t in range(KT):
                    act.wait_ge(s_xn, KT * j + t + 1)
                    full = sg[:, t % 2, 0:NP]
                    af(full, full, ACT.Identity, bias=mod[:, 8 * sh + t, 0:1], scale=mod[:, 8 * sc + t, 0:1]
                       ).then_inc(s_hf, 1)
                    act.wait_ge(s_hf, KT * j + t + 1)
                    nc.scalar.copy(h_hi[:, t, 0:NP], full).then_inc(s_hh, 1)

            act.dma_start(crow[0:1, :], A["c_prompt"]).then_inc(s_ld["c"], 16)
            act.dma_start(crow[1:9, :], A["c_sample"]).then_inc(s_ld["c"], 16)
            xp = A["x_prompt"][0].rearrange("(c p) d -> c p d", p=P)
            for c in range(4):
                act.dma_start(xtok[:, c, :], xp[c]).then_inc(s_ld["x"], 16)
            act.dma_start(xsrow, A["x_sample"].rearrange("b t d -> (b t) d")).then_inc(s_ld["xs"], 16)
            for name in VECS:
                v = A[name] if name == "norm_final" else A[name][0]
                r = v.shape[0] // P
                act.dma_start(vrow[VROW[name]:VROW[name] + r, :], v.rearrange("(r n) -> r n", n=P)
                              ).then_inc(s_ld["vec"], 16)
            act.dma_start(brow[0:72, :], A["b_ada"][0].rearrange("(r n) -> r n", n=P)).then_inc(s_ld["b"], 16)
            act.dma_start(brow[72:88, :], A["b_ada_final"].rearrange("(r n) -> r n", n=P)).then_inc(s_ld["b"], 16)
            cwr = A["conv_w"][0].rearrange("j (t n) -> (j t) n", n=P)
            for g in range(2):
                act.dma_start(cwrow[:, g, :], cwr[g * 124:(g + 1) * 124, :]).then_inc(s_ld["cw"], 16)

            ada_split(Lin(0))
            act.wait_ge(s_td, 1)
            act.wait_ge(s_tp, 1)
            af(c_f[:, :, 0:9], pg[:, 0, 0:80].rearrange("p (t n) -> p t n", n=10)[:, :, 0:9], ACT.Silu
               ).then_inc(s_te, 1)
            act.wait_ge(s_te, 1)
            nc.scalar.copy(c_hl[:, :, 0:10], c_f[:]).then_inc(s_c, 1)
            for t in range(KT):
                act.wait_ge(s_tp, 3 + t)
                nc.scalar.copy(x[:, t, 0:NP], pg[:, 2 + t % 2, :]).then_inc(s_te, 1)
            act.wait_ge(s_tp, 2 + KT)
            act.wait_ge(s_te, 1 + KT)
            act.wait_ge(s_td, 1 + KT)
            ada_split(Lin(1))
            ada_rows(Lin(0))
            ada_split(Lin(2))
            for t in range(KT):
                square(0, Lin(t), x)
            ada_rows(Lin(1))
            ada_split(Lin(3))
            rstd(1)
            for m in range(2, ADA0):
                ada_rows(Lin(m))
                if m + 2 < ADA0:
                    ada_split(Lin(m + 2))
                if m >= ADA0 - 2:
                    split_hi(Lin(m - (ADA0 - 2)), m % 2, 0)
            modulate(0, SC1, SH1)
            for m in range(ADA0, ADA0 + 2):
                ada_split(Lin(m))

            def ffn(which):
                def ada_part(c, m, i, last=False):
                    if which == 1 and c % 2 == 0:
                        ada_rows(Lin(m + c // 2, 2, i))
                        if not last:
                            ada_split(Lin(m + c // 2 + 2, 2, i))

                for g in range(3):
                    n0 = at[f"up{which}_{g}"]
                    a0 = (which - 1) * (FF // P) + sum(GROUPS[:g])
                    for i, k0 in bodies(act, GROUPS[g] // 2, n0 == 0):
                        for c in range(4):
                            n = Lin(n0 + 4 * k0 + c, 4, i)
                            hidden = lambda add: Lin(a0 + 2 * k0 + add, 2, i).value()
                            step(n)
                            if c < 2:
                                act.wait_ge(s_a, hidden(HIDDEN0))
                                af(halves(sg[:, c, :]), psum(c), ACT.Silu).then_inc(s_evac[c], 1)
                            else:
                                act.wait_ge(s_evac[c % 2], n.half().value(1, 1))
                                nc.scalar.copy(tile(f_hi, Lin(2 * k0 + c - 2, 2, i).value()), sg[:, c - 2, :]
                                               ).then_inc(s_ahi, 1)
                            ada_part(c, ADA_UP[g] + 2 * k0, i)
                    n0 = at[f"down{which}_{g}"]
                    if g == 2:
                        for c in range(8):
                            step(Lin(n0 + c), n0 + c + 2 < UNITS)
                            ada_part(c, ADA_DOWN[g], None, last=c // 4 == 1)
                            square((1, 4)[which - 1], Lin(c), x, s_x, (2, 6)[which - 1] * KT)
                    else:
                        with act.Fori(0, 2) as i:
                            for c in range(4):
                                step(Lin(n0 + c, 4, i))
                                ada_part(c, ADA_DOWN[g], i)

            ffn(1)
            rstd(2)
            modulate(1, SC2, SH2)
            def conv_units(i, n0, per):
                for c in range(4):
                    n = Lin(n0 + c, per, i)
                    step(n)
                    if c < 2:
                        if i is not None:
                            act.wait_ge(s_evac[c], n.half().value())
                        af(halves(sg[:, c, :]), psum(c), ACT.Sigmoid).then_inc(s_evac[c], 1)
                    elif i is None:
                        for t in range(4 * (c - 2), 4 * (c - 2) + 4):
                            act.wait_ge(s_cvt, t + 1)
                            nc.scalar.copy(sT[:, t, :, 0:TAPS - 1],
                                           pg[:, t % 4, 0:240].rearrange("p (b j) -> p b j", b=NS)
                                           ).then_inc(s_cve, 1)

            conv_units(None, at["conv"], 0)
            with act.Fori(0, 3) as i:
                conv_units(i, at["conv"] + 4, 4)
            n = at["alr"]
            act.wait_ge(s_done, n + 1)
            for e in (1, 0):
                nc.scalar.copy(alr[:, e * HALF:(e + 1) * HALF], pu[0][0:RANK, e, 0:HALF]).then_inc(s_evac[e], 2)
            for c in range(2):
                act.wait_ge(s_raw[1], Lin(n).half().half().value(16, 16))
                act.sem_inc(s_hi, 1)
            for c in range(2, 4):
                act.wait_ge(s_lo, n + c + 1)
                step(Lin(n + c))

            def z_out(h):
                act.wait_ge(s_lg, h + 1)
                b = 2 * (h % 2)
                af(halves(lb[:, h, :]), pg[:, b:b + 2, 0:HALF], ACT.Identity,
                   bias=vt[:, VROW["b_alpha"] + h:VROW["b_alpha"] + h + 1]).then_inc(s_z, 1)

            def log1p(heads):
                for h in heads:
                    act.wait_ge(s_az, h + 1)
                    w = sg[:, 2 + h % 2, :]
                    chain.mark(af(w, w, ACT.Exp, scale=-1.0))
                chain.wait()
                for h in heads:
                    w = sg[:, 2 + h % 2, :]
                    af(w, w, ACT.Ln, bias=ones[:, 0:1]).then_inc(s_l, 1)

            for i, k in bodies(act, 2, 1):
                for c in range(4):
                    step(Lin(at["qk"] + 4 * k + c, 4, i))
                    af(halves(tile(qk, Lin(2 * c + k, 1, i).value())), psum(c % 2), ACT.Copy,
                       scale=DK ** -0.5 if i is None else 1.0).then_inc(s_evac[c % 2], 1)
                    if i is None:
                        if c == 0:
                            act.wait_ge(s_ct, 1)
                            nc.scalar.copy(flat(sg[:])[0:38, 0:D].rearrange("p (e n) -> p e n", e=2), pg[0:38, 0:2, :]
                                           ).then_inc(s_cts, 1)
                        elif c < 3:
                            z_out(2 * c - 2)
                            z_out(2 * c - 1)
                        if c >= 2:
                            log1p((2 * c - 4, 2 * c - 3))
            act.wait_ge(s_cst, 32)
            act.wait_ge(s_b, HEADS)
            act.wait_ge(s_cvs, 1)
            act.wait_ge(s_xsp, 16)
            with act.Fori(0, 2) as i:
                for c in range(4):
                    step(Lin(at["v"] + c, 4, i))
                    nc.scalar.copy(halves(sg[:, c, :]), psum(c % 2)).then_inc(s_evac[c % 2], 1)
                    if c >= 2:
                        e = c - 2
                        act.wait_ge(s_vt, i * 2 + (e + 1))
                        f = i * 512 + 256 * e
                        nc.scalar.copy(vtok[:, :, bass.ds(f, DV)],
                                       pg[:, 0:2, :].rearrange("p a (c n) -> p (a c) n", c=2))
                        nc.scalar.copy(vs[:, bass.ds(f, DV)], pg[0:NS, 2, 0:DV]).then_inc(s_v, 1)

            def gate(i, c):
                n = Lin(at["gates"] + c, 12, i)
                p, j = c % 2, c % 4
                step(n)
                if c >= 4:
                    act.wait_ge(s_gsp[j], i * 48 + 16 * (c // 4))
                t = af(halves(sg[:, j, :]), psum(p), ACT.Tanh, scale=0.5)
                t.then_inc(s_gt if c < 4 else s_evac[p], 1)
                act.wait_ge(s_evac[p], n.half().value(1, 1))
                act.dma_start(gates_d[c // 4][bass.ds(i * 4 + j, 1)].rearrange("o p n -> (o p) n"), sg[:, j, :]
                              ).then_inc(s_gsp[j], 16)

            def exp(h, l):
                act.wait_ge(s_gd, h.value(8, l + 2))
                af(E_[:, l % 2, :], E_[:, l % 2, :], ACT.Exp, scale=1 / 16).then_inc(s_ge, 1)

            with act.Fori(0, 2) as i:
                for hh in range(2):
                    h = Lin(hh, 2, i)
                    for s in range(6):
                        gate(i, 6 * hh + s)
                        if s == 0:
                            af(EB, tile(lb, h.value()), ACT.Exp, scale=1 / 16).then_inc(s_ge, 1)
                            act.wait_ge(s_gd, h.value(8, 1))
                            af(E_[:, 0, :], E_[:, 0, :], ACT.Exp, scale=1 / 16).then_inc(s_ge, 1)
                            nc.scalar.copy(VH, vtok[:, :, bass.ds(h.value(DV), DV)]).then_inc(s_gk, 1)
                            exp(h, 0)
                            exp(h, 1)
                        if s == 1:
                            act.wait_ge(s_kt, h.value(1, 1))
                            nc.scalar.copy(KTK, pg[:, 2, :].rearrange("p (c n) -> p c n", c=NC)).then_inc(s_kr, 1)
                            nc.scalar.copy(ks8[:], pg[0:NS, 3, 0:DK]).then_inc(s_kr, 1)
                            exp(h, 2)
                            exp(h, 3)
                        if s == 2:
                            exp(h, 4)
                            exp(h, 5)
                        if s == 3:
                            exp(h, 6)
                        if s == 5:
                            dst = qk[:, bass.ds(h.value(2), 2), :]
                            act.wait_ge(s_o, h.value(2, 1))
                            nc.scalar.copy(dst[:, :, NP:N], pg[:, 2, 0:2 * NS].rearrange("p (t b) -> p t b", t=2)
                                           ).then_inc(s_oe, 1)
                            act.wait_ge(s_o, h.value(2, 2))
                            nc.scalar.copy(dst[:, :, 0:NP], pg[:, 2:4, :]).then_inc(s_oe, 1)
                for j in range(4):
                    act.wait_ge(s_gsp[j], i * 48 + 48)

            act.wait_ge(s_oe, 2 * HEADS)
            for h in range(HEADS):
                af(work_t[:, 2 * h:2 * h + 2, :], qk[:, 2 * h:2 * h + 2, :], ACT.Square).then_inc(s_osq, 1)
            for t in range(KT):
                square(2, Lin(t), d, s_cen)
            rstd(4)
            for t in range(KT):
                act.wait_ge(s_xn, 2 * KT + t + 1)
                af(d[:, t, :], d[:, t, :], ACT.Silu, scale=vt[:, VROW["conv_ln_g"] + t:VROW["conv_ln_g"] + t + 1],
                   bias=vt[:, VROW["conv_ln_b"] + t:VROW["conv_ln_b"] + t + 1]).then_inc(s_hf, 1)
                act.wait_ge(s_hf, 2 * KT + t + 1)
                nc.scalar.copy(h_hi[:, t, :], d[:, t, :]).then_inc(s_hh, 1)
            def o_roots(h):
                for j in (h, h + 1):
                    b = 2 * (j % 2)
                    act.wait_ge(s_os, j + 1)
                    af(halves(lb[:, j, :]), pg[:, b:b + 2, 0:HALF], ACT.Ln, scale=1 / DV, bias=eps[:]).then_inc(s_ol, 1)
                act.wait_ge(s_ol, h + 2)
                af(lb[:, h:h + 2, :], lb[:, h:h + 2, :], ACT.Exp, scale=-0.5).then_inc(s_om, 1)

            o_roots(0)
            for i, k in bodies(act, 2, 1):
                if i is None:
                    step(Lin(at["yconv"]))
                    step(Lin(at["yconv"] + 1))
                    o_roots(2)
                for c in range(4):
                    t = Lin(4 * k + c, 4, i)
                    if i is not None:
                        step(t + at["yconv"])
                    elif c % 2 == 0:
                        step(Lin(at["yconv"] + 2 + c // 2))
                    act.wait_ge(s_of, t.value(add=1))
                    nc.scalar.copy(tile(o_hi, t.value()), tile(qk, t.value())).then_inc(s_oh, 1)
            with act.Fori(0, 2) as i:
                for c in range(4):
                    step(Lin(at["ygla"] + c, 4, i))
                    act.wait_ge(s_mf, i * 4 + (c + 1))
                    nc.scalar.copy(tile(h_hi, i * 4 + c), sg[:, c % 2, :]).then_inc(s_mh, 1)
            for i, k in bodies(act, 2, 1):
                for c in range(4):
                    step(Lin(at["out"] + 4 * k + c, 4, i))
                    square(3, Lin(4 * k + c, 4, i), x, s_x, 3 * KT)
            rstd(5)
            modulate(3, SC3, SH3)
            ffn(2)
            rstd(6)
            for t in range(KT):
                act.wait_ge(s_xn, 4 * KT + t + 1)
                af(x[:, t, 0:NP], sg[:, t % 2, 0:NP], ACT.Identity, bias=mod[:, 8 * SHF + t, 0:1],
                   scale=mod[:, 8 * SCF + t, 0:1]).then_inc(s_yn, 1)
            act.wait_ge(s_yt, 1)
            nc.scalar.copy(ysrow.rearrange("p (e n) -> p e n", e=2), pu[0][0:NS, :, :]).then_inc(s_yse, 1)

        @block.vector
        def _(dve):
            V = nc.vector
            chain = Chain(dve, s_dv)
            conv = Chain(dve, s_cv)

            def split_lo(n, p, slot):
                dve.wait_ge(s_raw[slot], n.half().half().value(16, 16))
                dve.wait_ge(s_hi, n.value(1, 1))
                V.tensor_tensor(w_lo[p][:], raw[:, slot, :, p * P:(p + 1) * P], w_hi[p][:].bitcast(F32),
                                ALU.subtract).then_inc(s_lo, 1)

            def step(n, more=True):
                dve.wait_ge(s_done, n.value(1, 1))
                if more:
                    c = n.base % 4
                    split_lo(n + 2, c % 2, ((c + 2) // 2) % 2)

            def psum(p):
                return pu[p][:, :, 0:HALF]

            def part(j):
                return mod[:, 8 * j:8 * j + 8, :]

            def vec(r):
                return vt[:, r:r + KT].unsqueeze(2).to_broadcast([P, KT, 10])

            def ada_split(m):
                slot = m.base % 2
                dve.wait_ge(s_wah, m.value(1, 1))
                V.tensor_tensor(wa[slot][:, 1], ada_slot(m)[0], wa[slot][:, 0].bitcast(F32), ALU.subtract
                                ).then_inc(s_wal, 1)

            def ada_out(m):
                dve.wait_ge(s_at, m.value(1, 1))
                bias = vt[:, bass.ds(m.value(2, NVEC), 2)].unsqueeze(2).to_broadcast([P, 2, 10])
                V.tensor_tensor(mod[:, bass.ds(m.value(2), 2), :],
                                pg[:, m.base % 2, 0:20].rearrange("p (t c) -> p t c", t=2), bias, ALU.add
                                ).then_inc(s_mod, 1)

            def scale_of(j, gain):
                dve.wait_ge(s_mod, 4 * j + 4)
                chain.link(V.scalar_tensor_tensor(part(j), part(j), 1.0, vec(VROW[gain]), ALU.add, ALU.mult))

            def gate_of(j):
                dve.wait_ge(s_mod, 4 * j + 4)
                chain.link(V.tensor_scalar(part(j), part(j), 0.5, None, ALU.mult))

            def add_square(q, t):
                dve.wait_ge(s_sq, t.value(add=KT * q + 1))
                if t.i is None and t.base == 0:
                    V.tensor_copy(sg[:, 2, :], sg[:, 0, :]).then_inc(s_sqf, 1)
                else:
                    dve.wait_ge(s_sqf, t.value(add=KT * q))
                    V.tensor_tensor(sg[:, 2, :], sg[:, 2, :], sg[:, t.base % 2, :], ALU.add).then_inc(s_sqf, 1)

            def refine(r, ps, n):
                w = sg[:, 2, :]
                chain.link(V.tensor_tensor(w, r, r, ALU.mult))
                chain.link(V.scalar_tensor_tensor(halves(w), ps, n * EPS, halves(w), ALU.add, ALU.mult))
                chain.link(V.tensor_scalar(w, w, -0.5 / n, 1.5, ALU.mult, ALU.add))
                return V.tensor_tensor(r, r, w, ALU.mult)

            def rstd(j):
                dve.wait_ge(s_root, j)
                refine(sg[:, 3, :], pg[:, 0:2, 0:HALF], D).then_inc(s_rstd, 1)

            def modulate(j, sc, sh, final=False):
                if j:
                    rstd(j + 1)
                dve.wait_ge(s_rstd, j + 1)

                def samples():
                    rs = sg[:, 3, NP:N].unsqueeze(1).to_broadcast([P, KT, NS])
                    chain.link(V.tensor_tensor(hs[:], x[:, :, NP:N], rs, ALU.mult))
                    chain.link(V.tensor_tensor(hs[:], hs[:], part(sc)[:, :, 1:9], ALU.mult))
                    if final:
                        V.tensor_tensor(x[:, :, NP:N], hs[:], part(sh)[:, :, 1:9], ALU.add).then_inc(s_ys, 1)
                    else:
                        chain.link(V.tensor_tensor(hs[:], hs[:], part(sh)[:, :, 1:9], ALU.add))
                        chain.link(V.tensor_copy(h_hi[:, :, NP:N], hs[:]))
                        V.tensor_tensor(h_lo[:, :, NP:N], hs[:], h_hi[:, :, NP:N].bitcast(F32), ALU.subtract)

                def normed(t):
                    if final and t >= 2:
                        dve.wait_ge(s_yn, t - 1)
                    if not final and t >= 2:
                        dve.wait_ge(s_h, KT * j + t - 1)
                    V.tensor_tensor(sg[:, t % 2, 0:NP], x[:, t, 0:NP], sg[:, 3, 0:NP], ALU.mult).then_inc(s_xn, 1)

                def staged(t):
                    dve.wait_ge(s_yt, t + 2)
                    V.tensor_copy(ytok[:, :, t * P:(t + 1) * P], pg[:, t % 4, :].rearrange("p (c n) -> p c n", c=4)
                                  ).then_inc(s_ye, 1)

                normed(0)
                for t in range(KT):
                    if t + 1 < KT:
                        normed(t + 1)
                    if t == 0:
                        samples()
                    if final:
                        staged(t)
                    if not final:
                        dve.wait_ge(s_hh, KT * j + t + 1)
                        V.tensor_tensor(h_lo[:, t, 0:NP], sg[:, t % 2, 0:NP], h_hi[:, t, 0:NP].bitcast(F32),
                                        ALU.subtract).then_inc(s_h, 1)

            def residual(n, m, gt):
                p = n.base % 2
                g = lambda a, b: flat(mod[:, bass.ds(m + 8 * gt, 1), a:b])
                ps = pu[p]
                V.scalar_tensor_tensor(tile(x, m, 0, HALF), ps[:, 0, 0:HALF], g(0, 1), tile(x, m, 0, HALF),
                                       ALU.mult, ALU.add)
                V.scalar_tensor_tensor(tile(x, m, HALF, NP), ps[:, 1, 0:NP - HALF], g(0, 1), tile(x, m, HALF, NP),
                                       ALU.mult, ALU.add)
                V.tensor_tensor(t8[:, p, :], ps[:, 1, NP - HALF:HALF], g(1, 9), ALU.mult).then_inc(s_evac[p], 1)
                dve.wait_ge(s_evac[p], n.half().value(1, 1))
                V.tensor_tensor(tile(x, m, NP, N), tile(x, m, NP, N), t8[:, p, :], ALU.add).then_inc(s_x, 1)

            V.memset(c_f[:], 0.0).then_inc(s_cf, 1)
            V.memset(t8[:], 0.0).then_inc(s_a, HIDDEN0)
            dve.wait_ge(s_cf, 1)
            dve.wait_ge(s_tp, 2)
            V.tensor_copy(vt[:], pg[:, 1, 0:NVEC + NADA])
            V.tensor_copy(cw[:], pg[:, 1, 160:160 + TAPS * KT]).then_inc(s_td, 1)
            dve.wait_ge(s_c, 1)
            V.tensor_tensor(c_hl[:, :, 10:20], c_f[:], c_hl[:, :, 0:10].bitcast(F32), ALU.subtract).then_inc(s_c, 1)
            ada_split(Lin(0))
            for t in range(KT):
                dve.wait_ge(s_tp, 3 + t)
                V.tensor_copy(x[:, t, NP:N], pg[:, t % 2, 0:NS]).then_inc(s_td, 1)
            ada_split(Lin(1))
            ada_split(Lin(2))
            for t in range(KT):
                add_square(0, Lin(t))
            ada_split(Lin(3))
            rstd(1)
            for m in range(ADA0):
                if 2 <= m < ADA0 - 2:
                    ada_split(Lin(m + 2))
                ada_out(Lin(m))
                if m >= ADA0 - 2:
                    split_lo(Lin(m - (ADA0 - 2)), m % 2, 0)
            scale_of(SC1, "norm_ffn1")
            modulate(0, SC1, SH1)
            for m in range(ADA0, ADA0 + 2):
                ada_split(Lin(m))

            def ffn(which, gt):
                def ada_part(c, m, i, last=False):
                    if which == 1 and c % 2:
                        ada_out(Lin(m + c // 2, 2, i))
                    elif which == 1 and not last:
                        ada_split(Lin(m + c // 2 + 2, 2, i))

                a0 = (which - 1) * (FF // P)
                for g in range(3):
                    n0 = at[f"up{which}_{g}"]
                    a1 = a0 + sum(GROUPS[:g])
                    for i, k0 in bodies(dve, GROUPS[g] // 2, n0 == 0):
                        for c in range(4):
                            n = Lin(n0 + 4 * k0 + c, 4, i)
                            step(n)
                            if c >= 2:
                                p = c % 2
                                s = sg[:, p, :]
                                dve.wait_ge(s_evac[p], (n + (-2)).half().value(1, 1))
                                V.tensor_tensor(halves(s), halves(s), psum(p), ALU.mult).then_inc(s_evac[p], 1)
                                t = Lin(2 * k0 + p, 2, i)
                                dve.wait_ge(s_ahi, t.value(add=a1 + 1))
                                V.tensor_tensor(tile(f_lo, t.value()), s, tile(f_hi, t.value()).bitcast(F32),
                                                ALU.subtract).then_inc(s_a, 1)
                            ada_part(c, ADA_UP[g] + 2 * k0, i)
                    if g == 0:
                        gate_of(gt)
                    n0 = at[f"down{which}_{g}"]
                    if g == 2:
                        q = (1, 4)[which - 1]
                        for c in range(8):
                            step(Lin(n0 + c), n0 + c + 2 < UNITS)
                            residual(Lin(n0 + c), c, gt)
                            if c:
                                add_square(q, Lin(c - 1))
                            ada_part(c, ADA_DOWN[g], None, last=c // 4 == 1)
                        add_square(q, Lin(KT - 1))
                    else:
                        with dve.Fori(0, 2) as i:
                            for c in range(4):
                                n = Lin(n0 + c, 4, i)
                                step(n)
                                residual(n, i * 4 + c, gt)
                                ada_part(c, ADA_DOWN[g], i)

            ffn(1, GT1)
            scale_of(SC2, "norm_mix")
            gate_of(GT2)
            modulate(1, SC2, SH2)
            chain.link(V.memset(u[:, :, 0:TAPS - 1], 0.0))
            V.memset(SC, 0.0)

            def conv_first(pair):
                for t in (2 * pair, 2 * pair + 1):
                    conv.mark(V.tensor_scalar(d[:, t, 0:NP], u[:, t, 0:NP], cw[:, t:t + 1],
                                              vt[:, VROW["conv_b"] + t:VROW["conv_b"] + t + 1], ALU.mult, ALU.add))

            def conv_taps(pair, tap, count):
                for s in range(count):
                    for t in (2 * pair, 2 * pair + 1):
                        conv.wait(back=1)
                        conv.mark(V.scalar_tensor_tensor(
                            d[:, t, 0:NP], flat(u[:, t:t + 1, bass.ds(tap + s, NP)]),
                            cw[:, bass.ds((tap + s) * KT + t, 1)], d[:, t, 0:NP], ALU.mult, ALU.add))

            def conv_units(i, n0, per, t0, taps=False):
                for c in range(4):
                    n = Lin(n0 + c, per, i)
                    step(n)
                    if c >= 2:
                        p = c % 2
                        dve.wait_ge(s_evac[p], (n + (-2)).half().value(1, 1))
                        V.tensor_tensor(halves(tile(u, t0 + p, TAPS - 1, UP)), halves(sg[:, p, :]), psum(p),
                                        ALU.mult).then_inc(s_evac[p], 1)
                    if taps:
                        conv_taps(0, i * 10 + (1 + (0, 3, 6, 8)[c]), (3, 3, 2, 2)[c])

            conv_units(None, at["conv"], 0, 0)
            for p in range(2):
                dve.wait_ge(s_evac[p], (at["conv"] + 2) // 2 + 1)
            conv_first(0)
            with dve.Fori(0, 3) as i:
                conv.loop(i, 20)
                conv_units(i, at["conv"] + 4, 4, i * 2 + 2, taps=True)
            conv.end(3)
            n = at["alr"]
            for c in range(2):
                dve.wait_ge(s_raw[1], Lin(n).half().half().value(16, 16))
                dve.wait_ge(s_hi, n + 3 + c)
                dve.sem_inc(s_lo, 1)
            for c in range(2, 4):
                step(Lin(n + c))

            def sample_conv():
                dve.wait_ge(s_evac[0], at["alr"] // 2)
                dve.wait_ge(s_evac[1], at["alr"] // 2)
                dve.wait_ge(s_cve, KT)
                chain.link(V.tensor_copy(sT[:, :, :, TAPS - 1], u[:, :, UP - NS:UP]))
                taps = cw[:].rearrange("p (j t) -> p t j", t=KT)
                for t in range(KT):
                    chain.mark(V.tensor_tensor(sT[:, t], sT[:, t], taps[:, t:t + 1, :].to_broadcast([P, NS, TAPS]),
                                               ALU.mult))
                chain.wait()
                for t in range(KT):
                    chain.mark(V.tensor_reduce(d[:, t, NP:N], sT[:, t], AX_X, ALU.add))
                chain.wait()
                V.tensor_tensor(d[:, :, NP:N], d[:, :, NP:N],
                                vt[:, VROW["conv_b"]:VROW["conv_b"] + KT].unsqueeze(2).to_broadcast([P, KT, NS]),
                                ALU.add).then_inc(s_cvs, 1)

            def abs_z(h):
                dve.wait_ge(s_z, h + 1)
                z = lb[:, h, :]
                V.scalar_tensor_tensor(sg[:, 2 + h % 2, :], z, -1.0, z, ALU.mult, ALU.max).then_inc(s_az, 1)

            def decay(h):
                z = lb[:, h, :]
                dve.wait_ge(s_l, h + 1)
                chain.link(V.scalar_tensor_tensor(z, z, 0.0, sg[:, 2 + h % 2, :], ALU.min, ALU.subtract))
                for c in range(NC):
                    v = lb[:, h, c * CH:(c + 1) * CH]
                    last = V.tensor_tensor_scan(v, ones[:], v, 0.0, ALU.mult, ALU.add)
                last.then_inc(s_b, 1)

            conv_first(1)
            for c in range(4):
                step(Lin(at["qk"] + c))
                if c == 0:
                    sample_conv()
                if c == 1:
                    conv_taps(1, 1, 2)
                if c == 2:
                    abs_z(0)
                    abs_z(1)
                if c == 3:
                    for h in (0, 1):
                        decay(h)
                        abs_z(h + 2)
            for c in range(4):
                step(Lin(at["qk"] + 4 + c))
                conv_taps(1, 3 + 3 * c, 3)
                if c == 0:
                    decay(2)
                    decay(3)
            conv_first(2)
            with dve.Fori(0, 2) as i:
                conv.loop(i, 30)
                for c in range(4):
                    step(Lin(at["v"] + c, 4, i))
                    conv_taps(1, i * 8 + (15 + 2 * c), 2)
                    conv_taps(2, i * 7 + (1 + 2 * c), 2 if c < 3 else 1)
            conv.end(2)
            conv_first(3)

            def diff(h, l):
                w = LEVELS[l]
                blocks = lambda v: v.rearrange("p (b e t) -> p b e t", e=2, t=w)
                b, e = blocks(tile(lb, h.value(), 0, NP)), blocks(E_[:, l % 2, :])
                dve.wait_ge(s_gm, h.value(10, MIX[l - 2] if l >= 2 else MIX["k"]))
                mid = b[:, :, 0, w - 1:w].to_broadcast([P, NP // (2 * w), w])
                V.tensor_tensor(e[:, :, 1, :], b[:, :, 1, :], mid, ALU.subtract)
                V.tensor_tensor(e[:, :, 0, :], mid, b[:, :, 0, :], ALU.subtract).then_inc(s_gd, 1)

            def mix(h, l):
                w = LEVELS[l]
                blocks = lambda v: v.rearrange("p (b e t) -> p b e t", e=2, t=w)
                dve.wait_ge(s_ge, h.value(9, l + 3))
                if l >= 2:
                    dve.wait_ge(s_gg, h.value(8, l - 1))
                e, m = blocks(E_[:, l % 2, :]), blocks(M_[:, l % 2, 0:NP])
                q, k = (blocks(tile(qk, h.value(2, j), 0, NP)) for j in (0, 1))
                V.tensor_tensor(m[:, :, 1, :], e[:, :, 1, :], q[:, :, 1, :], ALU.mult)
                V.tensor_tensor(m[:, :, 0, :], e[:, :, 0, :], k[:, :, 0, :], ALU.mult).then_inc(s_gm, 1)

            def merge(h, l):
                if l:
                    dve.wait_ge(s_gp, h.value(8, l))
                    dve.sem_inc(s_merge, 1)
                V.copy_predicated(SC.rearrange("p (c t) -> p c t", c=NC),
                                  masks[:, l:l + 1, :].bitcast(U16).to_broadcast([P, NC, CH]),
                                  pg[:, l % 2, :].rearrange("p (c t) -> p c t", c=NC)).then_inc(s_gp, 1)

            def sample_states(h, r):
                dve.wait_ge(s_ko, h.value(2, r + 1))
                for b in range(4):
                    j = 4 * r + b
                    V.scalar_tensor_tensor(ST[:, j, :], ST[:, j, :], EB[:, NP + j:NP + j + 1],
                                           pg[:, 2 + b // 2, (b % 2) * DV:(b % 2 + 1) * DV],
                                           ALU.mult, ALU.add).then_inc(s_sn, 1)

            with dve.Fori(0, 2) as i:
                conv.loop(i, 46)
                chain.loop(i, 5)
                for hh in range(2):
                    h = Lin(hh, 2, i)
                    for s in range(6):
                        c = 6 * hh + s
                        n = Lin(at["gates"] + c, 12, i)
                        step(n)
                        if c < 4:
                            dve.wait_ge(s_gt, i * 4 + (c + 1))
                            V.scalar_tensor_tensor(halves(sg[:, c, :]), halves(sg[:, c, :]), 1.0, psum(c % 2),
                                                   ALU.add, ALU.mult).then_inc(s_evac[c % 2], 1)
                        if s == 0:
                            b = tile(lb, h.value(), 0, NP).rearrange("p (c t) -> p c t", c=NC)
                            end = b[:, :, CH - 1:CH].to_broadcast([P, NC, CH])
                            V.tensor_tensor(E_[:, 0, :].rearrange("p (c t) -> p c t", c=NC), end, b,
                                            ALU.subtract).then_inc(s_gd, 1)
                            dve.wait_ge(s_ge, h.value(9, 2))
                            V.tensor_copy(M_[:, 0, NP:N], tile(qk, h.value(2, 1), NP, N))
                            V.tensor_tensor(M_[:, 0, 0:NP], E_[:, 0, :], tile(qk, h.value(2, 1), 0, NP),
                                            ALU.mult).then_inc(s_gm, 1)
                            diff(h, 0)
                            diff(h, 1)
                        if s == 1:
                            dve.wait_ge(s_kt, h.value(1, 1))
                            V.tensor_tensor(QS, EB[:, 0:NP], tile(qk, h.value(2), 0, NP), ALU.mult).then_inc(s_gm, 1)
                            mix(h, 0)
                            diff(h, 2)
                            mix(h, 1)
                            diff(h, 3)
                            dve.wait_ge(s_kr, h.value(2, 2))
                            V.tensor_tensor(km, ks8[:].unsqueeze(1).to_broadcast([NS, NS, DK]),
                                            ident[0:NS, 0:NS].unsqueeze(2).to_broadcast([NS, NS, DK]),
                                            ALU.mult).then_inc(s_km, 1)
                        if s == 2:
                            dve.wait_ge(s_ds, h.value(1, 1))
                            dve.wait_ge(s_st, h.value(16, 16))
                            V.tensor_copy(SB[:, 0, :], pg[:, 2, 0:DV]).then_inc(s_S, 1)
                            for k in range(1, NC):
                                dve.wait_ge(s_S, h.value(4, k))
                                V.scalar_tensor_tensor(SB[:, k, :], SB[:, k - 1, :], EB[:, k * CH + CH - 1:(k + 1) * CH],
                                                       pg[:, 2 + k // 2, (k % 2) * DV:(k % 2 + 1) * DV],
                                                       ALU.mult, ALU.add).then_inc(s_S, 1)
                            mix(h, 2)
                            merge(h, 0)
                            diff(h, 4)
                            mix(h, 3)
                            merge(h, 1)
                            diff(h, 5)
                        if s == 3:
                            sample_states(h, 0)
                            mix(h, 4)
                            merge(h, 2)
                            diff(h, 6)
                            mix(h, 5)
                            merge(h, 3)
                        if s == 4:
                            sample_states(h, 1)
                            mix(h, 6)
                            merge(h, 4)
                            dve.wait_ge(s_gg, h.value(8, 6))
                            V.tensor_scalar(M_[:, 1, 0:NP], tile(qk, h.value(2, 1), 0, NP), 1.0, None, ALU.mult
                                            ).then_inc(s_gm, 1)
                            merge(h, 5)
                        if s == 5:
                            dve.wait_ge(s_gg, h.value(8, 8))
                            dve.sem_inc(s_merge, 1)
                            merge(h, 6)
                            merge(h, 7)
                        done, more = sum(TAPS_AT[:c]), sum(TAPS_AT[:c + 1])
                        conv_taps(2, i * 8 + (15 + sum(TAPS2_AT[:c])), TAPS2_AT[c])
                        conv_taps(3, i * 15 + (1 + done), more - done)
                        if c == 11:
                            for t in range(5):
                                chain.link(V.tensor_tensor(lb[:, 0, :], (d if t == 0 else lb)[:, 0, :],
                                                           d[:, t + 1, :], ALU.add))
            conv.end(2)
            chain.end(2)

            conv.wait()
            dve.wait_ge(s_gsp[2], 6 * 16)
            dve.wait_ge(s_gsp[3], 6 * 16)
            V.tensor_tensor(sg[:, 2, :], lb[:, 0, :], d[:, 6, :], ALU.add).then_inc(s_ln, 1)
            dve.wait_ge(s_ln, 1)
            V.tensor_tensor(sg[:, 2, :], sg[:, 2, :], d[:, 7, :], ALU.add).then_inc(s_ln, 1)
            dve.wait_ge(s_ss, 3)
            chain.link(V.tensor_scalar(halves(sg[:, 3, :]), pg[:, 0:2, 0:HALF], 1 / D, None, ALU.mult))

            def centered(t):
                V.tensor_tensor(d[:, t, :], d[:, t, :], sg[:, 3, :], ALU.subtract).then_inc(s_cen, 1)

            def scaled(t):
                V.tensor_tensor(d[:, t, :], d[:, t, :], sg[:, 3, :], ALU.mult).then_inc(s_xn, 1)

            centered(0)
            centered(1)
            for t in range(KT):
                if t + 2 < KT:
                    centered(t + 2)
                add_square(2, Lin(t))
            rstd(3)
            dve.wait_ge(s_rstd, 3)
            scaled(0)
            scaled(1)
            for t in range(KT):
                if t + 2 < KT:
                    scaled(t + 2)
                dve.wait_ge(s_hh, 2 * KT + t + 1)
                V.tensor_tensor(h_lo[:, t, :], d[:, t, :], h_hi[:, t, :].bitcast(F32), ALU.subtract).then_inc(s_h, 1)
            def o_rstd(h):
                dve.wait_ge(s_om, h // 2 + 1)
                if h:
                    dve.wait_ge(s_or, h)
                refine(lb[:, h, :], pg[:, 2 * (h % 2):2 * (h % 2) + 2, 0:HALF], DV).then_inc(s_or, 1)

            def yconv_unit(t):
                step(t + at["yconv"])
                m = halves(tile(work_t, t.value(add=KT)))
                V.scalar_tensor_tensor(m, m, 1.0, psum(t.base % 2), ALU.add, ALU.mult).then_inc(s_evac[t.base % 2], 1)

            o_rstd(0)
            o_rstd(1)
            gn = vt[:, VROW["gla_norm"]:VROW["gla_norm"] + KT]
            chain.link(V.tensor_scalar(gn, gn, 0.5, None, ALU.mult))
            dve.wait_ge(s_gr["gc"], 16)
            for i, k in bodies(dve, 2, 1):
                if i is None:
                    yconv_unit(Lin(0))
                    yconv_unit(Lin(1))
                    o_rstd(2)
                    o_rstd(3)
                    dve.wait_ge(s_or, HEADS)
                    dve.wait_ge(s_gr["r"], 16)
                for c in range(4):
                    t = Lin(4 * k + c, 4, i)
                    if i is not None:
                        yconv_unit(t)
                    elif c % 2 == 0:
                        yconv_unit(Lin(2 + c // 2))
                    ot = tile(qk, t.value())
                    V.tensor_tensor(ot, ot, tile(lb, Lin(2 * k + c // 2, 2, i).value()), ALU.mult).then_inc(s_ox, 1)
                    dve.wait_ge(s_ox, t.value(add=1))
                    V.scalar_tensor_tensor(ot, ot, vt[:, bass.ds(t.value(add=VROW["gla_norm"]), 1)],
                                           tile(d, t.value()), ALU.mult, ALU.mult).then_inc(s_of, 1)
                    dve.wait_ge(s_oh, t.value(add=1))
                    V.tensor_tensor(tile(o_lo, t.value()), ot, tile(o_hi, t.value()).bitcast(F32), ALU.subtract
                                    ).then_inc(s_osp, 1)
            dve.wait_ge(s_gr["gg"], 16)
            with dve.Fori(0, 2) as i:
                for c in range(4):
                    n = Lin(at["ygla"] + c, 4, i)
                    t = i * 4 + c
                    step(n)
                    s = sg[:, c % 2, :]
                    V.scalar_tensor_tensor(halves(s), halves(tile(work_t, t)), 1.0, psum(c % 2),
                                           ALU.add, ALU.mult).then_inc(s_evac[c % 2], 1)
                    dve.wait_ge(s_evac[c % 2], n.half().value(1, 1))
                    V.tensor_tensor(s, s, tile(work_t, t + KT), ALU.add).then_inc(s_mf, 1)
                    dve.wait_ge(s_mh, i * 4 + (c + 1))
                    V.tensor_tensor(tile(h_lo, t), s, tile(h_hi, t).bitcast(F32), ALU.subtract).then_inc(s_mp, 1)
            dve.wait_ge(s_xr, 16)
            for i, k in bodies(dve, 2, 1):
                for c in range(4):
                    n = Lin(at["out"] + 4 * k + c, 4, i)
                    step(n)
                    residual(n, Lin(4 * k + c, 4, i).value(), GT2)
                    if i is not None or c:
                        add_square(3, Lin(4 * k + c - 1, 4, i))
            add_square(3, Lin(KT - 1))
            scale_of(SC3, "norm_ffn2")
            modulate(3, SC3, SH3)
            ffn(2, GT3)
            scale_of(SCF, "norm_final")
            modulate(4, SCF, SHF, final=True)


_INS = ["x_prompt", "x_sample", "c_prompt", "c_sample", "state_conv", "state_gla", "w_ada", "b_ada", "norm_ffn1",
        "ffn1_gate", "ffn1_up", "ffn1_down", "norm_mix", "w_in", "conv_w", "conv_b", "conv_ln_g", "conv_ln_b",
        "w_conv_out", "w_alpha", "b_alpha", "gla_norm", "w_gla_out", "w_out", "norm_ffn2", "ffn2_gate", "ffn2_up",
        "ffn2_down", "norm_final", "w_ada_final", "b_ada_final"]
_OUTS = {"y_prompt": (1, NP, D), "y_sample": (NS, 1, D), "conv_p": (1, 1, TAPS - 1, D),
         "gla_p": (1, 1, HEADS, DK, DV), "conv_s": (1, NS, TAPS - 1, D), "gla_s": (1, NS, HEADS, DK, DV)}


def kernel(**inputs):
    import concourse.bacc as bacc
    from concourse.bass_utils import run_bass_kernel_spmd as run

    nc = bacc.Bacc("TRN2", target_bir_lowering=False, num_devices=1)
    arrays = {f"in_{k}": np.ascontiguousarray(inputs[k]) for k in _INS}
    a = {k: nc.dram_tensor(f"in_{k}", arrays[f"in_{k}"].shape, F32, kind="ExternalInput").ap() for k in _INS}
    o = {k: nc.dram_tensor(f"out_{k}", s, F32, kind="ExternalOutput").ap() for k, s in _OUTS.items()}
    decoder_step(nc, a, o)
    r = run(nc, [arrays], core_ids=[0])
    return tuple(r.results[0][f"out_{k}"] for k in _OUTS)
```
